# Optimizing a Trainium2 kernel written in Bass

```python
import jax, jax.numpy as jnp
from jax import lax
import numpy as np

D_MODEL = 2048
BATCH = 1
SEQ = 256
DEPTH = 2

N_EVEN = (DEPTH + 1) // 2
N_ODD = DEPTH // 2
MIX_WIDTH = D_MODEL

A_HEAD_DIM = 128
A_WIDTH = D_MODEL // 2
A_HEADS = A_WIDTH // A_HEAD_DIM
MOBA_BLOCK = 256
MOBA_TOPK = 3
MOBA_Q_CHUNK = 32
B_WIDTH = MIX_WIDTH - A_WIDTH
B_CONV = 3
AB_IN = 3 * A_WIDTH + 3 * B_WIDTH
C_WIDTH = D_MODEL // 2
C_BLOCKS = 8
C_BLOCK_DIM = C_WIDTH // C_BLOCKS
C_CONV = 4
RG_C = 8.0
D_WIDTH = MIX_WIDTH - C_WIDTH
D_HEADS = 4
D_HEAD_DIM = D_WIDTH // D_HEADS
MLSTM_CHUNK = 64
CD_IN = 2 * C_WIDTH + 4 * D_WIDTH + 2 * D_HEADS
FFN_HIDDEN = -(-8 * D_MODEL // (3 * 256)) * 256

EPS = 1e-6
NEG_INF = -1e30

kernel_name = "hybrid_moba_conv_rglru_mlstm_adaln"

def rmsnorm(x, g):
    xf = x.astype(jnp.float32)
    xf = xf * lax.rsqrt(jnp.mean(xf * xf, axis=-1, keepdims=True) + EPS)
    return xf.astype(x.dtype) * g

def alibi_slopes(n_heads):
    return 2.0 ** (-8.0 * jnp.arange(1, n_heads + 1, dtype=jnp.float32) / n_heads)

def causal_depthwise_conv(u, w):
    k_w, ch = w.shape
    return lax.conv_general_dilated(
        u, w[:, None, :].astype(u.dtype), window_strides=(1,), padding=[(k_w - 1, 0)],
        dimension_numbers=('NWC', 'WIO', 'NWC'), feature_group_count=ch)

def moba_attention(q, k, v, slopes):
    bsz, nh, s, dh = q.shape
    nb = -(-s // MOBA_BLOCK)
    pad = nb * MOBA_BLOCK - s
    kb = jnp.pad(k, ((0, 0), (0, 0), (0, pad), (0, 0))).reshape(bsz, nh, nb, MOBA_BLOCK, dh)
    vb = jnp.pad(v, ((0, 0), (0, 0), (0, pad), (0, 0))).reshape(bsz, nh, nb, MOBA_BLOCK, dh)
    scale = dh ** -0.5
    pos = jnp.arange(s, dtype=jnp.int32)
    q_block = pos // MOBA_BLOCK
    k_mean = jnp.mean(kb.astype(jnp.float32), axis=3)
    gate = jnp.einsum('bhsd,bhnd->bhsn', q.astype(jnp.float32), k_mean)
    fully_past = jnp.arange(nb)[None, :] < q_block[:, None]
    gate = jnp.where(fully_past, gate, NEG_INF)
    n_sel = min(MOBA_TOPK, nb)
    _, sel_idx = lax.top_k(gate, n_sel)
    sel_valid = sel_idx < q_block[None, None, :, None]
    b_ix = jnp.arange(bsz)[:, None, None, None]
    h_ix = jnp.arange(nh)[None, :, None, None]
    offs = jnp.arange(MOBA_BLOCK, dtype=jnp.int32)
    ql = MOBA_Q_CHUNK

    def chunk(ci):
        start = ci * ql
        qc = lax.dynamic_slice_in_dim(q, start, ql, axis=2)
        idx = lax.dynamic_slice_in_dim(sel_idx, start, ql, axis=2)
        ok = lax.dynamic_slice_in_dim(sel_valid, start, ql, axis=2)
        t = start + jnp.arange(ql, dtype=jnp.int32)
        k_sel = kb[b_ix, h_ix, idx]
        v_sel = vb[b_ix, h_ix, idx]
        own = start // MOBA_BLOCK
        k_own = lax.dynamic_index_in_dim(kb, own, axis=2, keepdims=False)
        v_own = lax.dynamic_index_in_dim(vb, own, axis=2, keepdims=False)
        s_sel = jnp.einsum('bhqd,bhqnkd->bhqnk', qc, k_sel).astype(jnp.float32) * scale
        dist_sel = (t[:, None, None] - (idx[..., None] * MOBA_BLOCK + offs)).astype(jnp.float32)
        s_sel = jnp.where(ok[..., None], s_sel - slopes[:, None, None, None] * dist_sel, NEG_INF)
        dist_own = (t[:, None] - (own * MOBA_BLOCK + offs)[None, :]).astype(jnp.float32)
        s_own = jnp.einsum('bhqd,bhkd->bhqk', qc, k_own).astype(jnp.float32) * scale
        s_own = jnp.where(dist_own >= 0, s_own - slopes[:, None, None] * dist_own, NEG_INF)
        scores = jnp.concatenate([s_sel.reshape(bsz, nh, ql, n_sel * MOBA_BLOCK), s_own], axis=-1)
        p = jax.nn.softmax(scores, axis=-1).astype(v.dtype)
        p_sel = p[..., :n_sel * MOBA_BLOCK].reshape(bsz, nh, ql, n_sel, MOBA_BLOCK)
        p_own = p[..., n_sel * MOBA_BLOCK:]
        return (jnp.einsum('bhqnk,bhqnkd->bhqd', p_sel, v_sel)
                + jnp.einsum('bhqk,bhkd->bhqd', p_own, v_own))

    out = lax.map(chunk, jnp.arange(s // ql))
    return out.transpose(1, 2, 0, 3, 4).reshape(bsz, nh, s, dh)

def _lin_combine(e1, e2):
    a1, b1 = e1
    a2, b2 = e2
    return a1 * a2, a2 * b1 + b2

def rglru(xc, wa, ba, wx, bx, lam):
    bsz, s, width = xc.shape
    xf = xc.astype(jnp.float32)
    xg = xf.reshape(bsz, s, C_BLOCKS, C_BLOCK_DIM)
    r = jax.nn.sigmoid(jnp.einsum('bsgi,gij->bsgj', xg, wa.astype(jnp.float32)).reshape(bsz, s, width) + ba)
    i = jax.nn.sigmoid(jnp.einsum('bsgi,gij->bsgj', xg, wx.astype(jnp.float32)).reshape(bsz, s, width) + bx)
    log_a = -RG_C * r * jax.nn.softplus(-lam.astype(jnp.float32))
    a = jnp.exp(log_a)
    u = jnp.sqrt(-jnp.expm1(2.0 * log_a)) * (i * xf)
    _, hs = lax.associative_scan(_lin_combine, (a, u), axis=1)
    return hs

def mlstm(q, k, v, i_pre, f_pre):
    bsz, nh, s, d = q.shape
    L = MLSTM_CHUNK
    nc = s // L
    k = k * d ** -0.5
    log_f = jax.nn.log_sigmoid(f_pre)
    to_chunks = lambda t: jnp.moveaxis(t.reshape(bsz, nh, nc, L, *t.shape[3:]), 2, 0)
    causal = jnp.tril(jnp.ones((L, L), dtype=bool))

    def step(carry, inp):
        C, n, m = carry
        qc, kc, vc, ic, lfc = inp
        b = jnp.cumsum(lfc, axis=-1)
        dmat = jnp.where(causal, b[..., :, None] - b[..., None, :] + ic[..., None, :], NEG_INF)
        inter = b + m[..., None]
        m_t = jnp.maximum(inter, jnp.max(dmat, axis=-1))
        w_intra = jnp.exp(dmat - m_t[..., None])
        w_inter = jnp.exp(inter - m_t)
        s_qk = jnp.einsum('bhld,bhsd->bhls', qc, kc) * w_intra
        num = (w_inter[..., None] * jnp.einsum('bhld,bhde->bhle', qc, C)
               + jnp.einsum('bhls,bhse->bhle', s_qk, vc))
        den = w_inter * jnp.einsum('bhld,bhd->bhl', qc, n) + jnp.sum(s_qk, axis=-1)
        h = num / jnp.maximum(jnp.abs(den), jnp.exp(-m_t))[..., None]
        b_last = b[..., -1]
        w_s = b_last[..., None] - b + ic
        m_new = jnp.maximum(b_last + m, jnp.max(w_s, axis=-1))
        decay = jnp.exp(b_last + m - m_new)
        ws = jnp.exp(w_s - m_new[..., None])
        C_new = decay[..., None, None] * C + jnp.einsum('bhs,bhsd,bhse->bhde', ws, kc, vc)
        n_new = decay[..., None] * n + jnp.einsum('bhs,bhsd->bhd', ws, kc)
        return (C_new, n_new, m_new), h

    init = (jnp.zeros((bsz, nh, d, d), jnp.float32), jnp.zeros((bsz, nh, d), jnp.float32),
            jnp.zeros((bsz, nh), jnp.float32))
    _, hs = lax.scan(step, init, (to_chunks(q), to_chunks(k), to_chunks(v),
                                  to_chunks(i_pre), to_chunks(log_f)))
    return jnp.moveaxis(hs, 0, 2).reshape(bsz, nh, s, d)

def mixer_ab(h, w_in, conv_w, w_out, slopes):
    bsz, s, _ = h.shape
    proj = h @ w_in
    q = proj[..., 0:A_WIDTH]
    k = proj[..., A_WIDTH:2 * A_WIDTH]
    v = proj[..., 2 * A_WIDTH:3 * A_WIDTH]
    o = 3 * A_WIDTH
    gate_b = proj[..., o:o + B_WIDTH]
    gate_c = proj[..., o + B_WIDTH:o + 2 * B_WIDTH]
    xb = proj[..., o + 2 * B_WIDTH:o + 3 * B_WIDTH]
    heads = lambda t: t.reshape(bsz, s, A_HEADS, A_HEAD_DIM).transpose(0, 2, 1, 3)
    ya = moba_attention(heads(q), heads(k), heads(v), slopes)
    ya = ya.transpose(0, 2, 1, 3).reshape(bsz, s, A_WIDTH)
    yb = gate_b * causal_depthwise_conv(gate_c * xb, conv_w)
    return jnp.concatenate([ya, yb], axis=-1) @ w_out

def mixer_cd(h, w_in, gate_bias, conv_w, conv_b, wa, ba, wx, bx, lam, w_out):
    bsz, s, _ = h.shape
    proj = h @ w_in
    x_rg = proj[..., 0:C_WIDTH]
    g_rg = proj[..., C_WIDTH:2 * C_WIDTH]
    o = 2 * C_WIDTH
    q = proj[..., o:o + D_WIDTH]
    k = proj[..., o + D_WIDTH:o + 2 * D_WIDTH]
    v = proj[..., o + 2 * D_WIDTH:o + 3 * D_WIDTH]
    og = proj[..., o + 3 * D_WIDTH:o + 4 * D_WIDTH]
    gates = (proj[..., o + 4 * D_WIDTH:] + gate_bias).astype(jnp.float32)
    i_pre = gates[..., :D_HEADS].transpose(0, 2, 1)
    f_pre = gates[..., D_HEADS:].transpose(0, 2, 1)
    xc = causal_depthwise_conv(x_rg, conv_w) + conv_b
    yc = rglru(xc, wa, ba, wx, bx, lam).astype(h.dtype) * jax.nn.gelu(g_rg)
    heads = lambda t: t.reshape(bsz, s, D_HEADS, D_HEAD_DIM).transpose(0, 2, 1, 3).astype(jnp.float32)
    hd = mlstm(heads(q), heads(k), heads(v), i_pre, f_pre)
    yd = hd.transpose(0, 2, 1, 3).reshape(bsz, s, D_WIDTH).astype(h.dtype) * jax.nn.sigmoid(og)
    return jnp.concatenate([yc, yd], axis=-1) @ w_out

def swiglu(h, w1, w3, w2):
    return (jax.nn.silu(h @ w1) * (h @ w3)) @ w2

def setup_inputs(seed: int = 0) -> dict:
    key = jax.random.key(seed)
    ks = jax.random.split(key, 24)
    f32 = jnp.float32
    D = D_MODEL

    def nrm(k, shape, scale):
        return jax.random.normal(k, shape, f32) * scale

    i_b = nrm(ks[13], (N_ODD, D_HEADS), 0.1)
    f_b = jnp.linspace(3.0, 6.0, D_HEADS, dtype=f32)[None, :] + nrm(ks[14], (N_ODD, D_HEADS), 0.1)
    u = jax.random.uniform(ks[21], (N_ODD, C_WIDTH), f32, 0.9, 0.999)
    a0 = u ** (1.0 / RG_C)
    return {
        "x": nrm(ks[0], (BATCH, SEQ, D), 1.0),
        "c": nrm(ks[1], (BATCH, D), 1.0),
        "mod_w": nrm(ks[2], (DEPTH, D, 6 * D), 0.5 * D ** -0.5),
        "mod_b": nrm(ks[3], (DEPTH, 6 * D), 0.02),
        "norm_mix_g": 1.0 + nrm(ks[4], (DEPTH, D), 0.02),
        "norm_ffn_g": 1.0 + nrm(ks[5], (DEPTH, D), 0.02),
        "ffn_w1": nrm(ks[6], (DEPTH, D, FFN_HIDDEN), D ** -0.5),
        "ffn_w3": nrm(ks[7], (DEPTH, D, FFN_HIDDEN), D ** -0.5),
        "ffn_w2": nrm(ks[8], (DEPTH, FFN_HIDDEN, D), FFN_HIDDEN ** -0.5),
        "ab_w_in": nrm(ks[9], (N_EVEN, D, AB_IN), D ** -0.5),
        "ab_conv_w": nrm(ks[10], (N_EVEN, B_CONV, B_WIDTH), B_CONV ** -0.5),
        "ab_w_out": nrm(ks[11], (N_EVEN, MIX_WIDTH, D), MIX_WIDTH ** -0.5),
        "cd_w_in": nrm(ks[12], (N_ODD, D, CD_IN), D ** -0.5),
        "cd_gate_b": jnp.concatenate([i_b, f_b], axis=-1),
        "rg_conv_w": nrm(ks[15], (N_ODD, C_CONV, C_WIDTH), C_CONV ** -0.5),
        "rg_conv_b": nrm(ks[16], (N_ODD, C_WIDTH), 0.02),
        "rg_wa": nrm(ks[17], (N_ODD, C_BLOCKS, C_BLOCK_DIM, C_BLOCK_DIM), C_BLOCK_DIM ** -0.5),
        "rg_ba": nrm(ks[18], (N_ODD, C_WIDTH), 0.02),
        "rg_wx": nrm(ks[19], (N_ODD, C_BLOCKS, C_BLOCK_DIM, C_BLOCK_DIM), C_BLOCK_DIM ** -0.5),
        "rg_bx": nrm(ks[20], (N_ODD, C_WIDTH), 0.02),
        "rg_lambda": jnp.log(a0) - jnp.log1p(-a0),
        "cd_w_out": nrm(ks[22], (N_ODD, MIX_WIDTH, D), MIX_WIDTH ** -0.5),
        "final_norm_g": 1.0 + nrm(ks[23], (D,), 0.02),
    }

def reference(x, c, mod_w, mod_b, norm_mix_g, norm_ffn_g, ffn_w1, ffn_w3, ffn_w2,
              ab_w_in, ab_conv_w, ab_w_out, cd_w_in, cd_gate_b, rg_conv_w, rg_conv_b,
              rg_wa, rg_ba, rg_wx, rg_bx, rg_lambda, cd_w_out, final_norm_g):
    slopes = alibi_slopes(A_HEADS)
    cond = jax.nn.silu(c)
    for layer in range(DEPTH):
        mod = cond @ mod_w[layer] + mod_b[layer]
        sh_m, sc_m, g_m, sh_f, sc_f, g_f = jnp.split(mod[:, None, :], 6, axis=-1)
        h = rmsnorm(x, norm_mix_g[layer]) * (1.0 + sc_m) + sh_m
        if layer % 2 == 0:
            e = layer // 2
            y = mixer_ab(h, ab_w_in[e], ab_conv_w[e], ab_w_out[e], slopes)
        else:
            o = layer // 2
            y = mixer_cd(h, cd_w_in[o], cd_gate_b[o], rg_conv_w[o], rg_conv_b[o], rg_wa[o],
                         rg_ba[o], rg_wx[o], rg_bx[o], rg_lambda[o], cd_w_out[o])
        x = x + g_m * y
        h = rmsnorm(x, norm_ffn_g[layer]) * (1.0 + sc_f) + sh_f
        x = x + g_f * swiglu(h, ffn_w1[layer], ffn_w3[layer], ffn_w2[layer])
    return rmsnorm(x, final_norm_g)


_drawn_inputs = setup_inputs


def setup_inputs(seed=0):
    import zlib

    import numpy as np

    out = dict(_drawn_inputs(seed))
    spreads = {}
    factors = {'rg_conv_b': 5.088, 'rg_ba': 64.0, 'rg_bx': 33.057, 'final_norm_g': 8.226}
    for name, (base, spread) in spreads.items():
        noise = np.random.default_rng([zlib.crc32(name.encode()), seed]).standard_normal(out[name].shape)
        drawn = base * np.exp(spread * noise) if base else spread * noise
        out[name] = __import__('jax').numpy.asarray(drawn.astype(out[name].dtype))
    for name, factor in factors.items():
        out[name] = (out[name] * factor).astype(out[name].dtype)
    return out
```

```python
from contextlib import ExitStack

import concourse.bass as bass
from concourse import mybir

F32 = mybir.dt.float32
F32R = mybir.dt.float32r
ALU = mybir.AluOpType
ACT = mybir.ActivationFunctionType
AX = mybir.AxisListType

P = 128
T = 256
D = 2048
KD = D // P
FFN = 5632
KF = FFN // P
HEADS_A = 8
HEADS_D = 4
TILES_D = 2
CHUNK_K = 2
GROUP = 4
RING = 4
MOD_GROUPS = 48
MOD_CHUNKS = KD // CHUNK_K
EPS = 1e-6

VECTORS = {}
_at = 0
for _name, _n in (("cond", KD), ("mod_b", 192), ("gain", 5 * KD), ("ab_conv", 24), ("rg_conv", 32),
                  ("rg_conv_b", 8), ("rg_ba", 8), ("rg_bx", 8), ("rg_lambda", 8), ("w_gates", KD * 8)):
    VECTORS[_name] = (_at, _at + _n)
    _at += _n
N_VECTORS = _at
TABLES = {}
_at = 0
for _name, _n in (("ident", P), ("ones", P)):
    TABLES[_name] = (_at, _at + _n)
    _at += _n
N_TABLES = _at


class Gemm:

    def __init__(self, kind, ktiles, bodies, first, rest, after=None):
        self.kind, self.bodies, self.first, self.rest = kind, bodies, first, rest
        self.n = ktiles // CHUNK_K
        self.chunk0 = after.chunk0 + after.bodies * 2 * after.n if after else 0
        self.tile0 = after.tile0 + after.bodies * 2 * GROUP if after else 0
        self.group0 = after.group0 + after.groups() if after else 8

    def groups(self):
        return self.first + (self.bodies - 1) * self.rest

    def chunks_before(self, i, half):
        return self.chunk0 + i * (2 * self.n) + half * self.n

    def tiles_before(self, i, half):
        return self.tile0 + i * (2 * GROUP) + half * GROUP

    def mods(self, first):
        return self.first if first else self.rest

    def groups_before(self, i, half, first):
        m = self.mods(first)
        inside = half * (m // 2)
        if first:
            return self.group0 + inside
        return self.group0 + self.first + (i - 1) * self.rest + inside

    def mod_chunk(self, half, j, first):
        m = self.mods(first)
        if m == 1 and j % 2 == 1:
            return 0, half * 4 + j // 2
        if m == 2:
            return 0, j
        if m == 4 and j < 8:
            return 0, j
        if m == 4 and 12 <= j < 20:
            return 1, j - 12
        return None

    def reduced_after(self, half, j, first):
        m = self.mods(first)
        if (m == 1 and half == 1 and j == 6) or (m == 2 and j == 6) or (m == 4 and j == 8):
            return 0
        if m == 4 and j == 20:
            return 1
        return None

    def carried(self, half, first):
        m = self.mods(first)
        return m == 2 or m == 4 or (m == 1 and half == 1)


def plan():
    ab = Gemm("store", KD, 6, 2, 2)
    ab_out = Gemm("residual", KD, 2, 0, 0, ab)
    up0 = Gemm("swiglu", KD, 11, 1, 1, ab_out)
    down0 = Gemm("residual", KF, 2, 4, 4, up0)
    cd = Gemm("store", KD, 6, 1, 1, down0)
    cd_out = Gemm("residual", KD, 2, 1, 1, cd)
    up1 = Gemm("swiglu", KD, 11, 1, 0, cd_out)
    down1 = Gemm("residual", KF, 2, 0, 0, up1)
    assert up1.group0 + up1.groups() == MOD_GROUPS
    return ab, ab_out, up0, down0, cd, cd_out, up1, down1


def wait(eng, sem, value):
    if not isinstance(value, int) or value > 0:
        eng.wait_ge(sem, value)


def trunk(nc, x_t, weights, mod_weights, vectors, tables, distances, futures, gate_b, rg_w, out_t):
    ab, ab_out, up0, down0, cd, cd_out, up1, down1 = plan()
    gemms = (ab, ab_out, up0, down0, cd, cd_out, up1, down1)

    with ExitStack() as ctx:
        def sb(name, shape, dt=F32):
            return ctx.enter_context(nc.sbuf_tensor(name, shape, dt))

        def sem(name):
            return ctx.enter_context(nc.semaphore(name))

        raw = sb("raw", [P, RING, CHUNK_K, GROUP * P])
        high = sb("high", [P, RING, CHUNK_K, GROUP * P], F32R)
        low = sb("low", [P, RING, CHUNK_K, GROUP * P], F32R)
        mod_raw = sb("mod_raw", [P, RING, CHUNK_K, GROUP * P])
        mod_acc = sb("mod_acc", [P, CHUNK_K, GROUP * P])
        mod = sb("mod", [P, 4 * MOD_GROUPS])
        x = sb("x", [P, KD, T])
        acts = sb("acts", [P, KD, 2, T], F32R)
        cross = sb("cross", [P, GROUP, T])
        summed = sb("summed", [P, GROUP, T])
        gate = sb("gate", [P, GROUP, T])
        vec = sb("vec", [P, N_VECTORS])
        tab = sb("tab", [P, N_TABLES])
        cond = sb("cond", [P, KD])
        norm_gain = sb("norm_gain", [P, KD])
        gates_w = sb("gates_w", [P, KD, 2, 8], F32R)
        small = sb("small", [P, 96])
        gbias = sb("gbias", [4, 2])
        with nc.sbuf_tensor("mixer", [P, 2 * KF, T], F32) as mixer:
            pass
        rms, inv_rms = mixer[:, 32], mixer[:, 33]
        hidden = sb("hidden", [P, KF, 2, T], F32R)

        bank = [ctx.enter_context(nc.psum_tensor(f"bank{b}", [P, 512], F32)) for b in range(8)]

        raw_landed = [sem(f"raw_landed{s}") for s in range(RING)]
        mod_landed = [sem(f"mod_landed{s}") for s in range(RING)]
        x_landed = sem("x_landed")
        constants_landed = sem("constants_landed")
        rg_landed = sem("rg_landed")
        out_landed = sem("out_landed")
        high_ready = sem("high_ready")
        low_ready = sem("low_ready")
        chunk_used = sem("chunk_used")
        cross_copied = sem("cross_copied")
        tile_out = sem("tile_out")
        x_updated = sem("x_updated")
        gate_ready = sem("gate_ready")
        hidden_ready = sem("hidden_ready")
        hidden_high = sem("hidden_high")
        hidden_low = sem("hidden_low")
        cond_ready = sem("cond_ready")
        mod_added = sem("mod_added")
        mod_reduced = sem("mod_reduced")
        mod_ready = sem("mod_ready")
        squared = sem("squared")
        square_sum = sem("square_sum")
        rms_ready = sem("rms_ready")
        inv_ready = sem("inv_ready")
        normed_ready = sem("normed_ready")
        norm_high = sem("norm_high")
        norm_low = sem("norm_low")
        normalised = sem("normalised")
        dve_step = sem("dve_step")
        act_step = sem("act_step")
        v_turned = sem("v_turned")
        v_stored = sem("v_stored")
        bias_ready = sem("bias_ready")
        scores_ready = sem("scores_ready")
        scores_max = sem("scores_max")
        probs_exp = sem("probs_exp")
        probs_ready = sem("probs_ready")
        probs_turned = sem("probs_turned")
        probs_stored = sem("probs_stored")
        heads_out = sem("heads_out")
        y_sums = sem("y_sums")
        y_high = sem("y_high")
        y_low = sem("y_low")
        gates_high = sem("gates_high")
        gates_split = sem("gates_split")
        gates_done = sem("gates_done")
        gates_copied = sem("gates_copied")
        gates_summed = sem("gates_summed")
        gates_rows = sem("gates_rows")
        f_rows = sem("f_rows")
        f_exp = sem("f_exp")
        f_exp1 = sem("f_exp1")
        f_log = sem("f_log")
        m_rows = sem("m_rows")
        m_exp = sem("m_exp")
        a_turned = sem("a_turned")
        a_stored = sem("a_stored")
        lam_exp = sem("lam_exp")
        lam_exp1 = sem("lam_exp1")
        lam_log = sem("lam_log")
        conv_ready = sem("conv_ready")
        rg_products = sem("rg_products")
        rg_sigmoid = sem("rg_sigmoid")
        log_a_ready = sem("log_a_ready")
        a_ready = sem("a_ready")
        u_square = sem("u_square")
        u_root = sem("u_root")
        gelu_ready = sem("gelu_ready")
        og_ready = sem("og_ready")
        m_spread = sem("m_spread")
        w_minus = sem("w_minus")
        w_exp = sem("w_exp")
        qk_ready = sem("qk_ready")
        p_ready = sem("p_ready")
        num_ready = sem("num_ready")
        den_abs = sem("den_abs")
        head_done = sem("head_done")

        def v(name):
            a, b = VECTORS[name]
            return vec[:, a:b]

        def t(name):
            a, b = TABLES[name]
            return tab[:, a:b]

        ident, ones = t("ident"), t("ones")
        gate_flat = gate[:].rearrange("p a t -> p (a t)")
        distance, future = gate_flat[:, 0:384], gate_flat[:, 0:384]
        select = gate_flat[0:4, 384:896].rearrange("p (h m) -> p h m", h=HEADS_D)
        gain = v("gain").rearrange("p (n j) -> p n j", j=KD)
        w_gates = v("w_gates").rearrange("p (k n) -> p k n", n=8)
        x_view = x_t.rearrange("(j p) t -> p j t", p=P)
        out_view = out_t.rearrange("(j p) t -> p j t", p=P)

        def mod_part(layer, part):
            c = (layer * 6 + part) * KD
            return mod[:, c:c + KD]

        def groups_for(layer, part):
            return (layer * 6 + part + 1) * 4

        def tiles(a, b):
            return mixer[:, a:b, :]

        def flat(a, b):
            return mixer[:, a:b, :].rearrange("p a t -> p (a t)")

        v_rows = mixer[:, 48:56, :].rearrange("p (s a) t -> p s (a t)", s=2)

        norms = ((0, 0, 0), (1, 0, 3), (2, 1, 0), (3, 1, 3))

        def rows4(n):
            return mixer[0:4, 64 + n, :]

        def mrows(n):
            return mixer[0:4, 72 + n, :]

        def decay(h):
            return mixer[:, 76 + 2 * (h % 2):78 + 2 * (h % 2), :].rearrange("p a t -> p (a t)")[:, 0:384]

        def den(h):
            return mixer[:, 80 + h % 2, :]

        def weighted(h):
            return mixer[:, 82 + 2 * (h % 2):84 + 2 * (h % 2), :].rearrange("p a t -> p (a t)")[:, 0:384]

        block = ctx.enter_context(nc.Block())

        @block.sync
        def _(sp):
            def load_raw(g_before, j):
                g = g_before + j
                wait(sp, low_ready, g - RING + 1)
                sp.dma_start(raw[:, j % RING], weights[bass.ds(g, 1)].rearrange(
                    "g p (k n) -> p (g k) n", k=CHUNK_K)).then_inc(raw_landed[j % RING], 16)

            def load_mod(g_before, j):
                g = g_before * MOD_CHUNKS + j
                wait(sp, mod_added, g - RING + 1)
                sp.dma_start(mod_raw[:, j % RING], mod_weights[bass.ds(g, 1)].rearrange(
                    "g p (k n) -> p (g k) n", k=CHUNK_K)).then_inc(mod_landed[j % RING], 16)

            sp.dma_start(vec[:], vectors).then_inc(constants_landed, 16)
            for j in range(MOD_CHUNKS):
                load_mod(0, j)
            sp.dma_start(tab[:], tables).then_inc(constants_landed, 16)
            sp.dma_start(gate_flat[:, 0:384], distances).then_inc(constants_landed, 16)
            sp.dma_start(gbias[:], gate_b).then_inc(constants_landed, 16)
            sp.dma_start(x[:], x_view).then_inc(x_landed, 16)
            with sp.Fori(1, 8) as i:
                for j in range(MOD_CHUNKS):
                    load_mod(i, j)

            def body(gm, i, first):
                for half in range(2):
                    c = gm.chunks_before(i, half)
                    off = (half * gm.n) % RING
                    for j in range(gm.n):
                        load_raw(c - off, j + off)
                        m = gm.mod_chunk(half, j, first)
                        if m:
                            load_mod(gm.groups_before(i, half, first) + m[0], m[1])

            for gm in gemms:
                if gm is cd:
                    wait(sp, tile_out, gm.tile0)
                    sp.dma_start(flat(56, 64), rg_w).then_inc(rg_landed, 16)
                    sp.dma_start(gate_flat[:, 0:896], futures).then_inc(rg_landed, 16)
                body(gm, 0, True)
                with sp.Fori(1, gm.bodies) as i:
                    body(gm, i, False)

            for q in range(4):
                sp.wait_ge(normalised, 4 * (q + 1))
                sp.dma_start(out_view[:, 4 * q:4 * q + 4], tiles(4 * q, 4 * q + 4)).then_inc(out_landed, 16)
            sp.wait_ge(out_landed, 64)

        @block.scalar
        def _(act):
            steps = [0]

            def link(ins):
                steps[0] += 1
                ins.then_inc(act_step, 1)
                act.wait_ge(act_step, steps[0])

            def split_high(c, j):
                g = c + j
                act.wait_ge(raw_landed[j % RING], landed_count(c, j))
                wait(act, chunk_used, g - RING + 1)
                nc.scalar.activation(high[:, j % RING], raw[:, j % RING], ACT.Copy).then_inc(high_ready, 1)

            def landed_count(c, j):
                return c * 4 + 16 * (j // RING + 1)

            def copy_cross(gm, i, half, f):
                tile = gm.tiles_before(i, half) + f
                wait(act, tile_out, tile - GROUP + 1)
                nc.scalar.copy(cross[:, f], bank[4 * half + f][:, T:2 * T]).then_inc(cross_copied, 1)

            def gate_silu(gm, i, f):
                act.wait_ge(tile_out, gm.tiles_before(i, 0) + f + 1)
                nc.scalar.activation(gate[:, f], gate[:, f], ACT.Silu).then_inc(gate_ready, 1)

            def hidden_split(gm, i, f):
                h0 = 0 if gm is up0 else KF
                act.wait_ge(hidden_ready, h0 + i * GROUP + f + 1)
                nc.scalar.activation(hidden[:, bass.ds(i * GROUP + f, 1), 0], summed[:, f:f + 1],
                                     ACT.Copy).then_inc(hidden_high, 1)

            def body(gm, i, first, done=0):
                for half in range(2):
                    c = gm.chunks_before(i, half)
                    off = (half * gm.n) % RING
                    before = None if first and half == 0 else (i, 0) if half else (i - 1, 1)
                    for j in range(gm.n):
                        if not (first and half == 0 and j < done):
                            split_high(c - off, j + off)
                        if before and 2 <= j < 2 + GROUP:
                            if j == 2:
                                act.wait_ge(chunk_used, c)
                            copy_cross(gm, *before, j - 2)
                        if before and gm.kind == "swiglu" and 3 <= j < 3 + GROUP:
                            if half:
                                gate_silu(gm, i, j - 3)
                            else:
                                hidden_split(gm, i - 1, j - 3)

            def gemm(gm, done):
                body(gm, 0, True, done)
                with act.Fori(1, gm.bodies) as i:
                    body(gm, i, False)
                last = gm.bodies - 1
                act.wait_ge(chunk_used, gm.chunks_before(last + 1, 0))
                for f in range(GROUP):
                    copy_cross(gm, last, 1, f)
                if gm.kind == "swiglu":
                    for f in range(GROUP):
                        hidden_split(gm, last, f)

            def first_chunks(gm):
                for j in range(RING):
                    split_high(gm.chunk0, j)

            def norm(n):
                with act.Fori(0, KD) as j:
                    nc.scalar.activation(mixer[:, bass.ds(j + KD, 1)], x[:, bass.ds(j, 1)],
                                         ACT.Square).then_inc(squared, 1)
                act.wait_ge(square_sum, n + 1)
                nc.scalar.activation(rms, bank[0][:, 0:T], ACT.Sqrt, bias=small[:, 95:96],
                                     scale=1.0 / D).then_inc(rms_ready, 1)
                if n < 4:
                    _, layer, part = norms[n]
                    shift = mod_part(layer, part)
                    with act.Fori(0, KD) as j:
                        act.wait_ge(normed_ready, n * KD + j + 1)
                        nc.scalar.activation(acts[:, bass.ds(j, 1), 0], mixer[:, bass.ds(j, 1)], ACT.Identity,
                                             bias=shift[:, bass.ds(j, 1)]).then_inc(norm_high, 1)

            act.wait_ge(constants_landed, 16)
            nc.scalar.activation(cond[:], v("cond"), ACT.Silu).then_inc(cond_ready, 1)
            act.wait_ge(x_landed, 16)
            act.wait_ge(dve_step, 1)

            first_chunks(ab)
            norm(0)
            gemm(ab, RING)
            first_chunks(ab_out)

            for b in range(4):
                act.wait_ge(v_turned, b + 1)
                nc.scalar.copy(v_rows[:, b // 2, 512 * (b % 2):512 * (b % 2) + 512], bank[4 + b][:]).then_inc(v_stored, 1)
            act.wait_ge(constants_landed, 64)
            for h in range(HEADS_A):
                slope = 2.0 ** (-8.0 * (h + 1) / HEADS_A)
                bias = mixer[:, 60 + 2 * (h % 2):62 + 2 * (h % 2), :].rearrange("p a t -> p (a t)")[:, 0:384]
                probs = mixer[:, 56 + 2 * (h % 2):58 + 2 * (h % 2), :].rearrange("p a t -> p (a t)")[:, 0:384]
                probs_t = mixer[:, 84 + 2 * (h % 2):86 + 2 * (h % 2), :].rearrange("p a t -> p (a t)")[:, 0:384]
                if h >= 2:
                    act.wait_ge(scores_max, h - 1)
                nc.scalar.mul(bias, distance, slope).then_inc(bias_ready, 1)
                act.wait_ge(scores_max, h + 1)
                nc.scalar.activation(probs[:, 0:128], probs[:, 0:128], ACT.Exp, bias=small[:, 2 * h:2 * h + 1],
                                     accum_out=small[:, 16 + 2 * h:17 + 2 * h]).then_inc(probs_exp, 1)
                nc.scalar.activation(probs[:, 128:384], probs[:, 128:384], ACT.Exp, bias=small[:, 2 * h + 1:2 * h + 2],
                                     accum_out=small[:, 17 + 2 * h:18 + 2 * h]).then_inc(probs_exp, 1)
                act.wait_ge(probs_turned, h + 1)
                nc.scalar.copy(probs_t, bank[2 + h % 2][:, 0:384]).then_inc(probs_stored, 1)
                act.wait_ge(heads_out, h + 1)
                nc.scalar.activation(acts[:, h, 0], bank[4 + h % 2][:, 0:T], ACT.Copy).then_inc(y_high, 1)
            act.wait_ge(conv_ready, 1)
            nc.scalar.activation(acts[:, 8:16, 0], tiles(72, 80), ACT.Copy).then_inc(y_high, 1)

            gemm(ab_out, RING)
            first_chunks(up0)
            act.wait_ge(x_updated, KD)
            norm(1)
            gemm(up0, RING)
            first_chunks(down0)
            gemm(down0, RING)
            first_chunks(cd)
            act.wait_ge(x_updated, 2 * KD)
            norm(2)
            gemm(cd, RING)
            first_chunks(cd_out)

            nc.scalar.activation(gates_w[:, :, 0], w_gates, ACT.Copy).then_inc(gates_high, 1)
            act.wait_ge(gates_done, 1)
            nc.scalar.copy(small[:, 0:32], bank[0][:, 0:32]).then_inc(gates_copied, 1)
            link(nc.scalar.activation(small[:, 32:40], v("rg_lambda"), ACT.Abs))
            nc.scalar.activation(small[:, 40:48], small[:, 32:40], ACT.Exp, scale=-1.0).then_inc(lam_exp, 1)
            act.wait_ge(lam_exp1, 1)
            nc.scalar.activation(small[:, 48:56], small[:, 40:48], ACT.Ln).then_inc(lam_log, 1)
            act.wait_ge(f_rows, 1)
            frow = rows4(3)
            link(nc.scalar.activation(frow, rows4(1), ACT.Abs))
            nc.scalar.activation(frow, frow, ACT.Exp, scale=-1.0).then_inc(f_exp, 1)
            act.wait_ge(f_exp1, 1)
            nc.scalar.activation(frow, frow, ACT.Ln).then_inc(f_log, 1)
            act.wait_ge(m_rows, 1)
            nc.scalar.activation(mrows(1), rows4(6), ACT.Exp, scale=-1.0).then_inc(m_exp, 1)
            for b in range(4):
                act.wait_ge(v_turned, 4 + b + 1)
                nc.scalar.copy(v_rows[:, b // 2, 512 * (b % 2):512 * (b % 2) + 512], bank[4 + b][:]).then_inc(v_stored, 1)
            for h in range(HEADS_D):
                act.wait_ge(w_minus, h + 1)
                nc.scalar.activation(decay(h), decay(h), ACT.Exp, scale=-1.0).then_inc(w_exp, 1)
                act.wait_ge(num_ready, h + 1)
                nc.scalar.activation(den(h), bank[2 + 4 * (h % 2)][:, 0:T], ACT.Abs).then_inc(den_abs, 1)
            nc.scalar.activation(tiles(40, 48), tiles(40, 48), ACT.Sigmoid).then_inc(og_ready, 1)
            act.wait_ge(y_sums, 1)
            nc.scalar.activation(acts[:, 8:16, 0], tiles(16, 24), ACT.Copy).then_inc(y_high, 1)
            for g in range(8):
                act.wait_ge(rg_products, g + 1)
                nc.scalar.activation(mixer[:, 72 + g], bank[g % 4][:, 0:T], ACT.Sigmoid,
                                     bias=v("rg_ba")[:, g:g + 1]).then_inc(rg_sigmoid, 1)
                nc.scalar.activation(mixer[:, 80 + g], bank[g % 4][:, T:2 * T], ACT.Sigmoid,
                                     bias=v("rg_bx")[:, g:g + 1]).then_inc(rg_sigmoid, 1)
            nc.scalar.activation(tiles(8, 16), tiles(8, 16), ACT.Gelu_apprx_tanh).then_inc(gelu_ready, 1)
            act.wait_ge(log_a_ready, 1)
            link(nc.scalar.activation(tiles(0, 8), tiles(72, 80), ACT.Exp))
            nc.scalar.activation(tiles(72, 80), tiles(72, 80), ACT.Tanh, scale=-1.0).then_inc(a_ready, 1)
            act.wait_ge(u_square, 1)
            nc.scalar.activation(tiles(64, 72), tiles(64, 72), ACT.Sqrt).then_inc(u_root, 1)
            act.wait_ge(y_sums, 2)
            nc.scalar.activation(acts[:, 0:8, 0], tiles(64, 72), ACT.Copy).then_inc(y_high, 1)

            gemm(cd_out, RING)
            first_chunks(up1)
            act.wait_ge(x_updated, 3 * KD)
            norm(3)
            gemm(up1, RING)
            first_chunks(down1)
            gemm(down1, RING)
            act.wait_ge(x_updated, 4 * KD)
            norm(4)

        @block.vector
        def _(dve):
            steps = [0]

            def link(ins):
                steps[0] += 1
                ins.then_inc(dve_step, 1)
                dve.wait_ge(dve_step, steps[0])

            def split_low(c, j):
                g = c + j
                dve.wait_ge(high_ready, g + 1)
                s = j % RING
                nc.vector.tensor_tensor(low[:, s], raw[:, s], high[:, s].bitcast(F32),
                                        ALU.subtract).then_inc(low_ready, 1)

            def add_mod(group, j):
                s = j % RING
                dve.wait_ge(mod_landed[s], group * 32 + 16 * (j // RING + 1))
                if j == 0:
                    wait(dve, mod_reduced, group)
                for k in range(CHUNK_K):
                    w, cs = mod_raw[:, s, k], cond[:, 2 * j + k:2 * j + k + 1]
                    if j == 0:
                        ins = nc.vector.tensor_scalar(mod_acc[:, k], w, cs, None, ALU.mult)
                    else:
                        if k == 0:
                            dve.wait_ge(mod_added, group * MOD_CHUNKS + j)
                        ins = nc.vector.scalar_tensor_tensor(mod_acc[:, k], w, cs, mod_acc[:, k], ALU.mult, ALU.add)
                ins.then_inc(mod_added, 1)

            def store_mod(group, b):
                dve.wait_ge(mod_reduced, group + 1)
                mb = v("mod_b")[:, bass.ds(group * 4, 4)]
                nc.vector.tensor_tensor(mod[:, bass.ds(group * 4, 4)], bank[b][:, 0:4], mb,
                                        ALU.add).then_inc(mod_ready, 1)

            def tile_done(gm, i, half, f):
                tile = gm.tiles_before(i, half) + f
                dve.wait_ge(cross_copied, tile + 1)
                main = bank[4 * half + f][:, 0:T]
                if gm.kind == "store":
                    nc.vector.tensor_tensor(mixer[:, bass.ds(i * 8 + 4 * half + f, 1)],
                                            cross[:, f:f + 1], main.rearrange("p (a t) -> p a t", a=1),
                                            ALU.add).then_inc(tile_out, 1)
                elif gm.kind == "residual":
                    layer = 0 if gm in (ab_out, down0) else 1
                    gates = mod_part(layer, 2 if gm in (ab_out, cd_out) else 5)
                    nc.vector.tensor_tensor(summed[:, f], cross[:, f], main, ALU.add).then_inc(tile_out, 1)
                    dve.wait_ge(tile_out, tile + 1)
                    n = i * 8 + 4 * half + f
                    xt = x[:, bass.ds(n, 1)]
                    nc.vector.scalar_tensor_tensor(xt, summed[:, f:f + 1], gates[:, bass.ds(n, 1)], xt,
                                                   ALU.mult, ALU.add).then_inc(x_updated, 1)
                elif half == 0:
                    nc.vector.tensor_tensor(gate[:, f], cross[:, f], main, ALU.add).then_inc(tile_out, 1)
                else:
                    nc.vector.tensor_tensor(summed[:, f], cross[:, f], main, ALU.add).then_inc(tile_out, 1)
                    dve.wait_ge(tile_out, tile + 1)
                    h0 = 0 if gm is up0 else KF
                    dve.wait_ge(gate_ready, h0 + i * GROUP + f + 1)
                    nc.vector.tensor_tensor(summed[:, f], summed[:, f], gate[:, f],
                                            ALU.mult).then_inc(hidden_ready, 1)

            def hidden_rest(gm, i, f):
                h0 = 0 if gm is up0 else KF
                dve.wait_ge(hidden_high, h0 + i * GROUP + f + 1)
                n = i * GROUP + f
                nc.vector.tensor_tensor(hidden[:, bass.ds(n, 1), 1], summed[:, f:f + 1],
                                        hidden[:, bass.ds(n, 1), 0].bitcast(F32),
                                        ALU.subtract).then_inc(hidden_low, 1)

            def body(gm, i, first, done=0):
                for half in range(2):
                    c = gm.chunks_before(i, half)
                    off = (half * gm.n) % RING
                    groups = gm.groups_before(i, half, first)
                    before = None if first and half == 0 else (i, 0) if half else (i - 1, 1)
                    if half:
                        carried = gm.carried(0, first)
                    else:
                        carried = before is not None and gm.carried(1, False)
                    for j in range(gm.n):
                        if not (first and half == 0 and j < done):
                            split_low(c - off, j + off)
                        if j == 2 and carried:
                            store_mod(groups - 1, 3 if half == 0 else 7)
                        if j == 12 and gm.mods(first) == 4:
                            store_mod(groups, 7 if half == 0 else 3)
                        if before and 2 <= j < 2 + GROUP:
                            tile_done(gm, *before, j - 2)
                        if before and gm.kind == "swiglu" and half == 0 and 4 <= j:
                            hidden_rest(gm, i - 1, j - 4)
                        m = gm.mod_chunk(half, j, first)
                        if m:
                            add_mod(groups + m[0], m[1])

            def gemm(gm, done):
                body(gm, 0, True, done)
                if gm.first and gm.first != gm.rest:
                    store_mod(gm.group0, 3)
                with dve.Fori(1, gm.bodies) as i:
                    body(gm, i, False)
                last = gm.bodies - 1
                if gm.rest:
                    store_mod(gm.group0 + gm.groups() - 1, 3)
                for f in range(GROUP):
                    tile_done(gm, last, 1, f)
                if gm.kind == "swiglu":
                    for f in range(GROUP):
                        hidden_rest(gm, last, f)

            def first_chunks(gm):
                for j in range(RING):
                    split_low(gm.chunk0, j)

            def norm(n):
                if n < 4:
                    index, layer, part = norms[n]
                    dve.wait_ge(mod_ready, groups_for(layer, part + 1))
                    link(nc.vector.scalar_tensor_tensor(norm_gain[:], mod_part(layer, part + 1), 1.0,
                                                        gain[:, index], ALU.add, ALU.mult))
                    gains = norm_gain[:]
                else:
                    gains = gain[:, n]
                dve.wait_ge(rms_ready, n + 1)
                nc.vector.reciprocal(inv_rms, rms).then_inc(inv_ready, 1)
                dve.wait_ge(inv_ready, n + 1)
                inv = inv_rms.rearrange("p (a t) -> p a t", a=1)
                with dve.Fori(0, KD) as j:
                    nc.vector.scalar_tensor_tensor(mixer[:, bass.ds(j, 1)], x[:, bass.ds(j, 1)],
                                                   gains[:, bass.ds(j, 1)], inv, ALU.mult,
                                                   ALU.mult).then_inc(normed_ready if n < 4 else normalised, 1)
                if n < 4:
                    shift = mod_part(layer, part)
                    with dve.Fori(0, KD) as j:
                        dve.wait_ge(norm_high, n * KD + j + 1)
                        nc.vector.scalar_tensor_tensor(acts[:, bass.ds(j, 1), 1], mixer[:, bass.ds(j, 1)],
                                                       shift[:, bass.ds(j, 1)],
                                                       acts[:, bass.ds(j, 1), 0].bitcast(F32),
                                                       ALU.add, ALU.subtract).then_inc(norm_low, 1)

            link(nc.vector.memset(small[:, 95:96], EPS))
            dve.wait_ge(constants_landed, 16)
            dve.wait_ge(cond_ready, 1)
            for j in range(MOD_CHUNKS):
                add_mod(0, j)
            store_mod(0, 3)
            with dve.Fori(1, 8) as i:
                for j in range(MOD_CHUNKS):
                    add_mod(i, j)
                store_mod(i, 3)
            first_chunks(ab)
            norm(0)
            gemm(ab, RING)
            first_chunks(ab_out)

            for h in range(HEADS_A):
                bias = mixer[:, 60 + 2 * (h % 2):62 + 2 * (h % 2), :].rearrange("p a t -> p (a t)")[:, 0:384]
                probs = mixer[:, 56 + 2 * (h % 2):58 + 2 * (h % 2), :].rearrange("p a t -> p (a t)")[:, 0:384]
                dve.wait_ge(scores_ready, h + 1)
                dve.wait_ge(bias_ready, h + 1)
                if h >= 2:
                    dve.wait_ge(probs_turned, h - 1)
                link(nc.vector.scalar_tensor_tensor(probs, bank[h % 2][:, 0:384], float(P) ** -0.5, bias,
                                                    ALU.mult, ALU.add))
                link(nc.vector.reduce_max(small[:, 2 * h:2 * h + 1], probs[:, 0:128], AX.X, negate=True))
                nc.vector.reduce_max(small[:, 2 * h + 1:2 * h + 2], probs[:, 128:384], AX.X,
                                     negate=True).then_inc(scores_max, 1)
                dve.wait_ge(probs_exp, 2 * h + 2)
                link(nc.vector.reciprocal(small[:, 32 + 2 * h:34 + 2 * h], small[:, 16 + 2 * h:18 + 2 * h]))
                link(nc.vector.tensor_scalar(probs[:, 0:128], probs[:, 0:128], small[:, 32 + 2 * h:33 + 2 * h],
                                             None, ALU.mult))
                nc.vector.tensor_scalar(probs[:, 128:384], probs[:, 128:384], small[:, 33 + 2 * h:34 + 2 * h],
                                        None, ALU.mult).then_inc(probs_ready, 1)
                dve.wait_ge(y_high, h + 1)
                nc.vector.tensor_tensor(acts[:, h, 1], bank[4 + h % 2][:, 0:T], acts[:, h, 0].bitcast(F32),
                                        ALU.subtract).then_inc(y_low, 1)
            taps = v("ab_conv").rearrange("p (g k) -> p g k", k=3)
            link(nc.vector.tensor_tensor(tiles(64, 72), tiles(32, 40), tiles(40, 48), ALU.mult))
            for g in range(8):
                u, y = mixer[:, 64 + g], mixer[:, 72 + g]
                link(nc.vector.tensor_scalar(y, u, taps[:, g, 2:3], None, ALU.mult))
                link(nc.vector.scalar_tensor_tensor(y[:, 1:T], u[:, 0:T - 1], taps[:, g, 1:2], y[:, 1:T],
                                                    ALU.mult, ALU.add))
                link(nc.vector.scalar_tensor_tensor(y[:, 2:T], u[:, 0:T - 2], taps[:, g, 0:1], y[:, 2:T],
                                                    ALU.mult, ALU.add))
            nc.vector.tensor_tensor(tiles(72, 80), tiles(72, 80), tiles(24, 32), ALU.mult).then_inc(conv_ready, 1)
            dve.wait_ge(conv_ready, 1)
            dve.wait_ge(y_high, 9)
            nc.vector.tensor_tensor(acts[:, 8:16, 1], tiles(72, 80), acts[:, 8:16, 0].bitcast(F32),
                                    ALU.subtract).then_inc(y_low, 1)

            gemm(ab_out, RING)
            first_chunks(up0)
            norm(1)
            gemm(up0, RING)
            first_chunks(down0)
            gemm(down0, RING)
            first_chunks(cd)
            norm(2)
            gemm(cd, RING)
            first_chunks(cd_out)

            dve.wait_ge(gates_high, 1)
            nc.vector.tensor_tensor(gates_w[:, :, 1], w_gates, gates_w[:, :, 0].bitcast(F32),
                                    ALU.subtract).then_inc(gates_split, 1)
            dve.wait_ge(gates_copied, 1)
            g4 = small[:, 0:32].rearrange("p (s b n) -> p s b n", s=2, b=2)
            nc.vector.tensor_tensor(small[:, 64:80].rearrange("p (s n) -> p s n", s=2), g4[:, :, 0], g4[:, :, 1],
                                    ALU.add).then_inc(gates_summed, 1)
            dve.wait_ge(lam_exp, 1)
            nc.vector.tensor_scalar(small[:, 40:48], small[:, 40:48], 1.0, None, ALU.add).then_inc(lam_exp1, 1)
            dve.wait_ge(lam_log, 1)
            link(nc.vector.tensor_scalar(small[:, 32:40], v("rg_lambda"), -1.0, 0.0, ALU.mult, ALU.max))
            link(nc.vector.tensor_tensor(small[:, 32:40], small[:, 32:40], small[:, 48:56], ALU.add))
            link(nc.vector.tensor_scalar(small[:, 32:40], small[:, 32:40], -8.0, None, ALU.mult))
            dve.wait_ge(gates_rows, 1)
            link(nc.vector.tensor_scalar(rows4(0), bank[1][0:4, 0:T], gbias[0:4, 0:1], None, ALU.add))
            nc.vector.tensor_scalar(rows4(1), bank[1][0:4, T:2 * T], gbias[0:4, 1:2], None,
                                    ALU.add).then_inc(f_rows, 1)
            dve.wait_ge(f_exp, 1)
            nc.vector.tensor_scalar(rows4(3), rows4(3), 1.0, None, ALU.add).then_inc(f_exp1, 1)
            dve.wait_ge(f_log, 1)
            link(nc.vector.scalar_tensor_tensor(rows4(2), rows4(1), 0.0, rows4(3), ALU.min, ALU.subtract))
            link(nc.vector.memset(rows4(7), 1.0))
            link(nc.vector.tensor_tensor_scan(rows4(4), rows4(7), rows4(2), 0.0, ALU.mult, ALU.add))
            link(nc.vector.tensor_tensor(rows4(5), rows4(0), rows4(4), ALU.subtract))
            link(nc.vector.tensor_tensor_scan(mrows(0), rows4(5), rows4(5), 0.0, ALU.max, ALU.max))
            nc.vector.tensor_tensor(rows4(6), rows4(4), mrows(0), ALU.add).then_inc(m_rows, 1)
            dve.wait_ge(a_turned, 1)
            nc.vector.tensor_copy(small[:, 80:88], bank[1][:, 0:8]).then_inc(a_stored, 1)
            dve.wait_ge(a_stored, 1)
            for h in range(HEADS_D):
                spread = bank[0 + 4 * (h % 2)]
                dve.wait_ge(m_spread, h + 1)
                link(nc.vector.scalar_tensor_tensor(decay(h)[:, 0:256], spread[:, 0:256], small[:, 80 + h:81 + h],
                                                    future[:, 0:256], ALU.subtract, ALU.add))
                nc.vector.scalar_tensor_tensor(decay(h)[:, 256:384], spread[:, 128:256], small[:, 84 + h:85 + h],
                                               future[:, 256:384], ALU.subtract, ALU.add).then_inc(w_minus, 1)
                dve.wait_ge(w_exp, h + 1)
                dve.wait_ge(qk_ready, h + 1)
                if h >= 2:
                    dve.wait_ge(num_ready, h - 1)
                nc.vector.scalar_tensor_tensor(weighted(h), bank[1 + 4 * (h % 2)][:, 0:384], 1.0 / 16.0, decay(h),
                                               ALU.mult, ALU.mult).then_inc(p_ready, 1)
                dve.wait_ge(den_abs, h + 1)
                link(nc.vector.tensor_tensor(den(h), den(h), spread[:, 256:512], ALU.max))
                link(nc.vector.reciprocal(den(h), den(h)))
                for e in range(TILES_D):
                    ins = nc.vector.tensor_tensor(mixer[:, 16 + 2 * h + e], bank[3 + 4 * (h % 2)][:, e * T:e * T + T],
                                                  den(h), ALU.mult)
                    if e == 0:
                        link(ins)
                    else:
                        ins.then_inc(head_done, 1)
            dve.wait_ge(head_done, HEADS_D)
            dve.wait_ge(og_ready, 1)
            nc.vector.tensor_tensor(tiles(16, 24), tiles(16, 24), tiles(40, 48), ALU.mult).then_inc(y_sums, 1)
            dve.wait_ge(y_sums, 1)
            dve.wait_ge(y_high, 10)
            nc.vector.tensor_tensor(acts[:, 8:16, 1], tiles(16, 24), acts[:, 8:16, 0].bitcast(F32),
                                    ALU.subtract).then_inc(y_low, 1)

            rtaps = v("rg_conv").rearrange("p (g k) -> p g k", k=4)
            for g in range(8):
                u, y = mixer[:, g], mixer[:, 64 + g]
                link(nc.vector.tensor_scalar(y, u, rtaps[:, g, 3:4], v("rg_conv_b")[:, g:g + 1], ALU.mult, ALU.add))
                for k in range(2, -1, -1):
                    s = 3 - k
                    ins = nc.vector.scalar_tensor_tensor(y[:, s:T], u[:, 0:T - s], rtaps[:, g, k:k + 1], y[:, s:T],
                                                         ALU.mult, ALU.add)
                    if k:
                        link(ins)
                    else:
                        ins.then_inc(conv_ready, 1)
            dve.wait_ge(conv_ready, 9)
            for g in range(8):
                dve.wait_ge(rg_sigmoid, 2 * g + 2)
                ins = nc.vector.tensor_scalar(mixer[:, 72 + g], mixer[:, 72 + g], small[:, 32 + g:33 + g], None,
                                              ALU.mult)
                if g < 7:
                    link(ins)
                else:
                    ins.then_inc(log_a_ready, 1)
            link(nc.vector.tensor_tensor(tiles(80, 88), tiles(80, 88), tiles(64, 72), ALU.mult))
            dve.wait_ge(a_ready, 1)
            link(nc.vector.tensor_tensor(tiles(64, 72), tiles(0, 8), tiles(0, 8), ALU.mult))
            nc.vector.scalar_tensor_tensor(flat(64, 72), flat(64, 72), 1.0, flat(72, 80), ALU.add,
                                           ALU.mult).then_inc(u_square, 1)
            dve.wait_ge(u_root, 1)
            link(nc.vector.tensor_tensor(tiles(64, 72), tiles(64, 72), tiles(80, 88), ALU.mult))
            for g in range(8):
                link(nc.vector.tensor_tensor_scan(mixer[:, 72 + g], mixer[:, g], mixer[:, 64 + g], 0.0,
                                                  ALU.mult, ALU.add))
            dve.wait_ge(gelu_ready, 1)
            nc.vector.tensor_tensor(tiles(64, 72), tiles(72, 80), tiles(8, 16), ALU.mult).then_inc(y_sums, 1)
            dve.wait_ge(y_sums, 2)
            dve.wait_ge(y_high, 11)
            nc.vector.tensor_tensor(acts[:, 0:8, 1], tiles(64, 72), acts[:, 0:8, 0].bitcast(F32),
                                    ALU.subtract).then_inc(y_low, 1)

            gemm(cd_out, RING)
            first_chunks(up1)
            norm(3)
            gemm(up1, RING)
            first_chunks(down1)
            gemm(down1, RING)
            norm(4)

        @block.tensor
        def _(pe):
            def sum_mod(group, b):
                pe.wait_ge(mod_added, (group + 1) * MOD_CHUNKS)
                for f in range(4):
                    for k in range(CHUNK_K):
                        ins = pe.matmul(bank[b][:, f:f + 1], mod_acc[:, k, f * P:f * P + P], ones[:, 0:1],
                                        start=(k == 0), stop=(k == CHUNK_K - 1))
                ins.then_inc(mod_reduced, 1)

            def body(gm, i, first, operand, landed, count0):
                for half in range(2):
                    c = gm.chunks_before(i, half)
                    off = (half * gm.n) % RING
                    groups = gm.groups_before(i, half, first)
                    for j in range(gm.n):
                        pe.wait_ge(low_ready, c + j + 1)
                        if first and half == 0 and landed is not None:
                            pe.wait_ge(landed, count0(j))
                        s = (j + off) % RING
                        for f in range(GROUP):
                            b = bank[4 * half + f]
                            if j == 0:
                                wait(pe, tile_out, gm.tiles_before(i, half) + f - 2 * GROUP + 1)
                                if f == GROUP - 1:
                                    pe.wait_ge(mod_ready, groups)
                            for k in range(CHUNK_K):
                                kt = CHUNK_K * j + k
                                wl, wh = low[:, s, k, f * P:f * P + P], high[:, s, k, f * P:f * P + P]
                                last = kt == CHUNK_K * gm.n - 1
                                if last:
                                    pe.matmul(b[:, T:2 * T], wl, operand[:, kt, 0], start=False, stop=False)
                                ins = pe.matmul(b[:], wh, operand[:, kt].rearrange("p a t -> p (a t)"),
                                                start=(kt == 0), stop=last)
                                if not last:
                                    ins = pe.matmul(b[:, T:2 * T], wl, operand[:, kt, 0], start=False, stop=False)
                        ins.then_inc(chunk_used, 1)
                        r = gm.reduced_after(half, j, first)
                        if r is not None:
                            sum_mod(groups + r, 7 if half == 0 else 3)

            def gemm(gm, operand, landed, count0):
                body(gm, 0, True, operand, landed, count0)
                with pe.Fori(1, gm.bodies) as i:
                    body(gm, i, False, operand, landed, count0)

            def norm(n):
                for j in (0,):
                    pe.wait_ge(squared, n * KD + 1)
                    pe.matmul(bank[0][:, 0:T], ones, mixer[:, KD], start=True, stop=False)
                with pe.Fori(1, KD - 1) as j:
                    pe.wait_ge(squared, n * KD + j + 1)
                    pe.matmul(bank[0][:, 0:T], ones, mixer[:, bass.ds(j + KD, 1)], start=False, stop=False)
                pe.wait_ge(squared, n * KD + KD)
                pe.matmul(bank[0][:, 0:T], ones, mixer[:, 2 * KD - 1], start=False,
                          stop=True).then_inc(square_sum, 1)

            def turn_values(first_tile, done):
                for b in range(4):
                    for q in range(4):
                        src = mixer[:, first_tile + 4 * (b % 2) + q, P * (b // 2):P * (b // 2) + P]
                        ins = pe.transpose(bank[4 + b][:, q * P:q * P + P], src, ident)
                    ins.then_inc(v_turned, 1)

            pe.wait_ge(constants_landed, 64)
            sum_mod(0, 3)
            with pe.Fori(1, 8) as i:
                pe.wait_ge(mod_ready, i)
                sum_mod(i, 3)
            norm(0)
            pe.wait_ge(rms_ready, 1)
            gemm(ab, acts, norm_low, lambda j: 2 * j + 2)

            pe.wait_ge(tile_out, ab_out.tile0)
            turn_values(16, 0)
            for h in range(HEADS_A + 1):
                if h < HEADS_A:
                    if h >= 2:
                        pe.wait_ge(scores_max, h - 1)
                    q, k = mixer[:, h], mixer[:, 8 + h]
                    pe.matmul(bank[h % 2][:, 0:128], q[:, 0:P], k[:, 0:P], start=True, stop=True)
                    pe.matmul(bank[h % 2][:, 128:384], q[:, P:T], k, start=True, stop=True).then_inc(scores_ready, 1)
                if h >= 1:
                    g = h - 1
                    probs = mixer[:, 56 + 2 * (g % 2):58 + 2 * (g % 2), :].rearrange("p a t -> p (a t)")[:, 0:384]
                    probs_t = mixer[:, 84 + 2 * (g % 2):86 + 2 * (g % 2), :].rearrange("p a t -> p (a t)")[:, 0:384]
                    pe.wait_ge(probs_ready, g + 1)
                    if g >= 2:
                        pe.wait_ge(probs_stored, g - 1)
                    for q in range(3):
                        ins = pe.transpose(bank[2 + g % 2][:, q * P:q * P + P], probs[:, q * P:q * P + P], ident)
                    ins.then_inc(probs_turned, 1)
                    pe.wait_ge(probs_stored, g + 1)
                    pe.wait_ge(v_stored, 4)
                    if g >= 2:
                        pe.wait_ge(y_low, g - 1)
                    o = bank[4 + g % 2]
                    pe.matmul(o[:, 0:T], v_rows[:, 0, g * P:g * P + P], probs_t[:, 0:256], start=True, stop=False)
                    pe.matmul(o[:, P:T], v_rows[:, 1, g * P:g * P + P], probs_t[:, 256:384], start=False,
                              stop=True).then_inc(heads_out, 1)
            gemm(ab_out, acts, y_low, lambda j: min(2 * j + 2, 8) + j // 4)
            norm(1)
            pe.wait_ge(rms_ready, 2)
            gemm(up0, acts, norm_low, lambda j: KD + 2 * j + 2)
            gemm(down0, hidden, hidden_low, lambda j: 2 * j + 2)
            norm(2)
            pe.wait_ge(rms_ready, 3)
            gemm(cd, acts, norm_low, lambda j: 2 * KD + 2 * j + 2)

            pe.wait_ge(tile_out, cd_out.tile0)
            pe.wait_ge(gates_split, 1)
            for s in range(2):
                for k in range(KD):
                    gp = bank[0][:, 16 * s:16 * s + 16]
                    last = k == KD - 1
                    pe.matmul(gp, acts[:, k, 0, s * P:s * P + P], gates_w[:, k].rearrange("p a n -> p (a n)"),
                              start=(k == 0), stop=False)
                    ins = pe.matmul(gp[:, 0:8], acts[:, k, 1, s * P:s * P + P], gates_w[:, k, 0], start=False,
                                    stop=last)
            ins.then_inc(gates_done, 1)
            turn_values(32, 4)
            pe.wait_ge(gates_summed, 1)
            for n in range(2):
                for s in range(2):
                    ins = pe.matmul(bank[1][0:4, n * T + s * P:n * T + s * P + P],
                                    small[:, 64 + 8 * s + 4 * n:68 + 8 * s + 4 * n], ident, start=True, stop=True)
            ins.then_inc(gates_rows, 1)
            pe.wait_ge(m_rows, 1)
            for s in range(2):
                ins = pe.matmul(bank[1][:, 4 * s:4 * s + 4], rows4(5)[:, s * P:s * P + P], ident[0:4, 0:4],
                                start=True, stop=True)
            ins.then_inc(a_turned, 1)
            pe.wait_ge(m_exp, 1)
            pe.wait_ge(rg_landed, 32)
            pe.wait_ge(a_stored, 1)
            pe.wait_ge(v_stored, 8)
            for h in range(HEADS_D):
                b = 4 * (h % 2)
                if h >= 2:
                    pe.wait_ge(head_done, h - 1)
                for n in range(2):
                    ins = pe.matmul(bank[b][:, n * T:n * T + T], select[0:4, h], mrows(n), start=True, stop=True)
                ins.then_inc(m_spread, 1)
                for d in range(TILES_D):
                    q, k = mixer[:, 16 + 2 * h + d], mixer[:, 24 + 2 * h + d]
                    pe.matmul(bank[b + 1][:, 0:256], k[:, 0:P], q, start=(d == 0), stop=(d == 1))
                for d in range(TILES_D):
                    q, k = mixer[:, 16 + 2 * h + d], mixer[:, 24 + 2 * h + d]
                    ins = pe.matmul(bank[b + 1][:, 256:384], k[:, P:T], q[:, P:T], start=(d == 0), stop=(d == 1))
                ins.then_inc(qk_ready, 1)
                pe.wait_ge(p_ready, h + 1)
                w = weighted(h)
                pe.matmul(bank[b + 2][:, 0:T], ones, w[:, 0:256], start=True, stop=False)
                pe.matmul(bank[b + 2][:, P:T], ones, w[:, 256:384], start=False, stop=True)
                for e in range(TILES_D):
                    c = (2 * h + e) * P
                    o = bank[b + 3][:, e * T:e * T + T]
                    pe.matmul(o, v_rows[:, 0, c:c + P], w[:, 0:256], start=True, stop=False)
                    ins = pe.matmul(o[:, P:T], v_rows[:, 1, c:c + P], w[:, 256:384], start=False, stop=True)
                ins.then_inc(num_ready, 1)
            rg = flat(56, 64).rearrange("p (n g j) -> p n g j", n=2, g=8)
            pe.wait_ge(rg_landed, 32)
            pe.wait_ge(head_done, HEADS_D)
            for g in range(8):
                pe.wait_ge(conv_ready, 1 + g + 1)
                if g >= 4:
                    pe.wait_ge(rg_sigmoid, 2 * (g - 3))
                for n in range(2):
                    ins = pe.matmul(bank[g % 4][:, n * T:n * T + T], rg[:, n, g], mixer[:, 64 + g],
                                    start=True, stop=True)
                ins.then_inc(rg_products, 1)

            gemm(cd_out, acts, y_low, lambda j: 9 + 2)
            norm(3)
            pe.wait_ge(rms_ready, 4)
            gemm(up1, acts, norm_low, lambda j: 3 * KD + 2 * j + 2)
            gemm(down1, hidden, hidden_low, lambda j: KF + 2 * j + 2)
            norm(4)


def _chunks(w):
    k, n = w.shape
    return w.reshape(k // 256, 2, 128, n // 512, 512).transpose(3, 0, 2, 1, 4).reshape(n // 512, k // 256, 128, 1024)


def kernel(**inputs):
    import numpy as np
    import concourse.bacc as bacc
    from concourse.bass_utils import run_bass_kernel_spmd

    a = {k: np.asarray(w) for k, w in inputs.items()}

    def columns(vector):
        return vector.reshape(-1, 128).T

    def flat_chunks(w):
        return _chunks(w).reshape(-1, 128, 1024)

    def pairs(w1, w3):
        return np.stack([_chunks(w1), _chunks(w3)], axis=1).reshape(-1, 128, 1024)

    cd_w = a["cd_w_in"][0]
    gates_at = cd_w.shape[1] - 8
    weights = np.concatenate([
        flat_chunks(a["ab_w_in"][0]), flat_chunks(a["ab_w_out"][0]),
        pairs(a["ffn_w1"][0], a["ffn_w3"][0]), flat_chunks(a["ffn_w2"][0]),
        flat_chunks(cd_w[:, :gates_at]), flat_chunks(a["cd_w_out"][0]),
        pairs(a["ffn_w1"][1], a["ffn_w3"][1]), flat_chunks(a["ffn_w2"][1]),
    ])
    mod_weights = np.concatenate([flat_chunks(a["mod_w"][0]), flat_chunks(a["mod_w"][1])])
    vectors = np.concatenate([
        columns(a["c"][0]), columns(a["mod_b"].reshape(-1)),
        columns(np.concatenate([a["norm_mix_g"][0], a["norm_ffn_g"][0], a["norm_mix_g"][1],
                                a["norm_ffn_g"][1], a["final_norm_g"]])),
        a["ab_conv_w"][0].reshape(3, 8, 128).transpose(2, 1, 0).reshape(128, 24),
        a["rg_conv_w"][0].reshape(4, 8, 128).transpose(2, 1, 0).reshape(128, 32),
        columns(a["rg_conv_b"][0]), columns(a["rg_ba"][0]), columns(a["rg_bx"][0]), columns(a["rg_lambda"][0]),
        cd_w[:, gates_at:].reshape(16, 128, 8).transpose(1, 0, 2).reshape(128, 128),
    ], axis=1)
    gate_b = np.ascontiguousarray(a["cd_gate_b"].reshape(2, 4).T)
    rg_w = np.stack([a["rg_wa"][0], a["rg_wx"][0]]).transpose(2, 0, 1, 3).reshape(128, 2048)

    n = np.arange(128)
    back = n[:, None] - n[None, :]
    causal = np.where(back >= 0, -back, -1e34).astype(np.float32)
    distance = np.concatenate([causal, -(back + 128).astype(np.float32), causal], axis=1)
    later = np.where(n[:, None] > n[None, :], 1e30, 0.0).astype(np.float32)
    future = np.concatenate([later, np.zeros((128, 128), np.float32), later], axis=1)
    select = np.zeros((128, 4, 128), np.float32)
    for h in range(4):
        select[h, h] = 1.0
    tables = np.concatenate([np.eye(128, dtype=np.float32), np.ones((128, 128), np.float32)], axis=1)
    futures = np.concatenate([future, select.reshape(128, 512)], axis=1)

    arrays = {"x_t": a["x"][0].T, "weights": weights, "mod_weights": mod_weights, "vectors": vectors,
              "tables": tables, "distances": distance, "futures": futures, "gate_b": gate_b, "rg_w": rg_w}
    arrays = {k: np.ascontiguousarray(w) for k, w in arrays.items()}
    nc = bacc.Bacc("TRN2", target_bir_lowering=False, num_devices=1, dynamic_dma_scratch_size=1024)
    args = [nc.dram_tensor(k, w.shape, F32, kind="ExternalInput").ap() for k, w in arrays.items()]
    out = nc.dram_tensor("out_t", (D, T), F32, kind="ExternalOutput").ap()
    trunk(nc, *args, out)
    r = run_bass_kernel_spmd(nc, [arrays], core_ids=[0])
    return np.ascontiguousarray(r.results[0]["out_t"].T)[None]
```

```python
from contextlib import ExitStack

import concourse.bass as bass
from concourse import mybir

F32 = mybir.dt.float32
F32R = mybir.dt.float32r
ALU = mybir.AluOpType
ACT = mybir.ActivationFunctionType
AX = mybir.AxisListType

P = 128
T = 256
D = 2048
KD = D // P
FFN = 5632
KF = FFN // P
HEADS_A = 8
HEADS_D = 4
TILES_D = 2
CHUNK_K = 2
GROUP = 4
RING = 4
MOD_GROUPS = 48
MOD_CHUNKS = KD // CHUNK_K
EPS = 1e-6

VECTORS = {}
_at = 0
for _name, _n in (("cond", KD), ("mod_b", 192), ("gain", 5 * KD), ("ab_conv", 24), ("rg_conv", 32),
                  ("rg_conv_b", 8), ("rg_ba", 8), ("rg_bx", 8), ("rg_lambda", 8), ("w_gates", KD * 8)):
    VECTORS[_name] = (_at, _at + _n)
    _at += _n
N_VECTORS = _at
TABLES = {}
_at = 0
for _name, _n in (("ident", P), ("ones", T)):
    TABLES[_name] = (_at, _at + _n)
    _at += _n
N_TABLES = _at


class Gemm:

    def __init__(self, kind, ktiles, mods, loop=None, after=None, drained=False, fed=None):
        self.kind, self.bodies, self.mods, self.loop = kind, len(mods), mods, loop
        self.n = ktiles // CHUNK_K
        self.before = after if not drained else None
        self.fed = fed
        self.quad0 = after.quad0 + after.bodies * after.n // 2 if after else 0
        self.tile0 = after.tile0 + after.bodies * 2 * GROUP if after else 0
        self.group0 = after.group0 + sum(after.mods) if after else 8

    def parts(self):
        lo, hi = self.loop or (self.bodies, self.bodies)
        return [*range(lo), *([(lo, hi)] if self.loop else []), *range(hi, self.bodies)]

    def m(self, i):
        return self.mods[i] if isinstance(i, int) else self.mods[self.loop[0]]

    def offset(self, half):
        return (half * self.n) % RING

    def quads(self, i, half):
        return self.quad0 + i * (self.n // 2) + (half * self.n - self.offset(half)) // RING

    def tiles(self, i, half):
        return self.tile0 + i * (2 * GROUP) + half * GROUP

    def groups(self, i, half):
        m = self.m(i)
        inside = half * (m // 2)
        if isinstance(i, int):
            return self.group0 + sum(self.mods[:i]) + inside
        lo = self.loop[0]
        return self.group0 + sum(self.mods[:lo]) + (i - lo) * m + inside

    def mod_chunk(self, i, half, j):
        m = self.m(i)
        if m == 1 and j % 2 == 1:
            return 0, half * 4 + j // 2
        if m == 2:
            return 0, j
        if m == 4 and j < 8:
            return 0, j
        if m == 4 and 12 <= j < 20:
            return 1, j - 12
        return None

    def reduced_after(self, i, half, j):
        m = self.m(i)
        if (m == 1 and half == 1 and j == 6) or (m == 2 and j == 6) or (m == 4 and j == 8):
            return 0
        if m == 4 and j == 20:
            return 1
        return None

    def carries(self, i, half):
        return self.m(i) in (2, 4) or (self.m(i) == 1 and half == 1)

    def previous(self, i, half):
        if half:
            return (self, i, 0), self.carries(i, 0)
        if isinstance(i, int) and i == 0:
            if self.before is None:
                return None, False
            last = self.before.bodies - 1
            return (self.before, last, 1), self.before.carries(last, 1)
        before = i - 1 if isinstance(i, int) else self.loop[0] - 1
        return (self, i - 1, 1), self.carries(before, 1)


def plan():
    ab = Gemm("store", KD, [2, 2, 2, 1, 1, 1], loop=(1, 3), fed=0)
    ab_out = Gemm("residual", KD, [2, 1], after=ab, fed=1)
    up0 = Gemm("swiglu", KD, [1] * 11, loop=(2, 11), after=ab_out, drained=True, fed=2)
    down0 = Gemm("residual", KF, [4, 4], after=up0)
    cd = Gemm("store", KD, [1] * 6, after=down0, drained=True, fed=3)
    cd_out = Gemm("residual", KD, [1, 1], after=cd, fed=4)
    up1 = Gemm("swiglu", KD, [1] + [0] * 10, loop=(2, 11), after=cd_out, drained=True, fed=5)
    down1 = Gemm("residual", KF, [0, 0], after=up1)
    assert up1.group0 + sum(up1.mods) == MOD_GROUPS
    return ab, ab_out, up0, down0, cd, cd_out, up1, down1


def wait(eng, sem, value):
    if not isinstance(value, int) or value > 0:
        eng.wait_ge(sem, value)


def trunk(nc, x_t, weights, mod_weights, vectors, tables, distances, futures, gate_b, rg_w, out_t):
    ab, ab_out, up0, down0, cd, cd_out, up1, down1 = plan()
    gemms = (ab, ab_out, up0, down0, cd, cd_out, up1, down1)

    with ExitStack() as ctx:
        def sb(name, shape, dt=F32):
            return ctx.enter_context(nc.sbuf_tensor(name, shape, dt))

        def sem(name):
            return ctx.enter_context(nc.semaphore(name))

        raw = sb("raw", [P, RING, CHUNK_K, GROUP * P])
        high = sb("high", [P, RING, CHUNK_K, GROUP * P], F32R)
        low = sb("low", [P, RING, CHUNK_K, GROUP * P], F32R)
        mod_raw = sb("mod_raw", [P, RING, CHUNK_K, GROUP * P])
        mod_acc = sb("mod_acc", [P, CHUNK_K, GROUP * P])
        mod = sb("mod", [P, 4 * MOD_GROUPS])
        x = sb("x", [P, KD, T])
        acts = sb("acts", [P, KD, 2, T], F32R)
        cross = sb("cross", [P, GROUP, T])
        summed = sb("summed", [P, GROUP, T])
        gate = sb("gate", [P, GROUP, T])
        vec = sb("vec", [P, N_VECTORS])
        tab = sb("tab", [P, N_TABLES])
        cond = sb("cond", [P, KD])
        norm_gain = sb("norm_gain", [P, KD])
        gates_w = sb("gates_w", [P, KD, 2, 8], F32R)
        small = sb("small", [P, 97])
        gbias = sb("gbias", [4, 2])
        with nc.sbuf_tensor("mixer", [P, 2 * KF, T], F32) as mixer:
            pass
        hidden = sb("hidden", [P, KF, 2, T], F32R)

        bank = [ctx.enter_context(nc.psum_tensor(f"bank{b}", [P, 512], F32)) for b in range(8)]

        raw_landed = [sem(f"raw_landed{s}") for s in range(RING)]
        mod_landed = [sem(f"mod_landed{s}") for s in range(RING)]
        x_landed = sem("x_landed")
        vectors_landed = sem("vectors_landed")
        tables_landed = sem("tables_landed")
        rg_landed = sem("rg_landed")
        futures_landed = sem("futures_landed")
        out_landed = sem("out_landed")
        high_ready = sem("high_ready")
        low_ready = sem("low_ready")
        low_ready_pool = sem("low_ready_pool")
        chunk_used = sem("chunk_used")
        cross_copied = sem("cross_copied")
        tile_out = sem("tile_out")
        x_updated = sem("x_updated")
        x_squared = sem("x_squared")
        squares_added = sem("squares_added")
        gate_ready = sem("gate_ready")
        hidden_ready = sem("hidden_ready")
        hidden_high = sem("hidden_high")
        hidden_low = sem("hidden_low")
        cond_ready = sem("cond_ready")
        mod_added = sem("mod_added")
        mod_reduced = sem("mod_reduced")
        mod_ready = sem("mod_ready")
        square_sum = sem("square_sum")
        rms_ready = sem("rms_ready")
        normed_ready = sem("normed_ready")
        feed_high = sem("feed_high")
        feed_low = sem("feed_low")
        normalised = sem("normalised")
        dve_step = sem("dve_step")
        act_step = sem("act_step")
        v_turned = sem("v_turned")
        v_stored = sem("v_stored")
        bias_ready = sem("bias_ready")
        scores_ready = sem("scores_ready")
        scores_max = sem("scores_max")
        probs_exp = sem("probs_exp")
        probs_ready = sem("probs_ready")
        probs_turned = sem("probs_turned")
        probs_stored = sem("probs_stored")
        heads_out = sem("heads_out")
        heads_stored = sem("heads_stored")
        conv_ready = sem("conv_ready")
        gates_high = sem("gates_high")
        gates_split = sem("gates_split")
        gates_done = sem("gates_done")
        gates_copied = sem("gates_copied")
        gates_summed = sem("gates_summed")
        gates_rows = sem("gates_rows")
        f_rows = sem("f_rows")
        f_exp = sem("f_exp")
        f_exp1 = sem("f_exp1")
        f_log = sem("f_log")
        m_rows = sem("m_rows")
        m_exp = sem("m_exp")
        a_turned = sem("a_turned")
        a_stored = sem("a_stored")
        lam_exp = sem("lam_exp")
        lam_exp1 = sem("lam_exp1")
        lam_log = sem("lam_log")
        rg_conv_ready = sem("rg_conv_ready")
        rg_products = sem("rg_products")
        rg_sigmoid = sem("rg_sigmoid")
        log_a_ready = sem("log_a_ready")
        a_ready = sem("a_ready")
        u_square = sem("u_square")
        u_root = sem("u_root")
        gelu_ready = sem("gelu_ready")
        rg_y_ready = sem("rg_y_ready")
        og_ready = sem("og_ready")
        m_spread = sem("m_spread")
        w_minus = sem("w_minus")
        w_exp = sem("w_exp")
        qk_ready = sem("qk_ready")
        p_ready = sem("p_ready")
        num_ready = sem("num_ready")
        den_abs = sem("den_abs")
        head_done = sem("head_done")
        mlstm_y_ready = sem("mlstm_y_ready")

        def v(name):
            a, b = VECTORS[name]
            return vec[:, a:b]

        def t(name):
            a, b = TABLES[name]
            return tab[:, a:b]

        ident, ones = t("ident"), t("ones")[:, 0:P]
        gate_flat = gate[:].rearrange("p a t -> p (a t)")
        distance, future = gate_flat[:, 0:384], gate_flat[:, 0:384]
        select = gate_flat[0:4, 384:896].rearrange("p (h m) -> p h m", h=HEADS_D)
        square, square_acc = gate[:, 0:2], gate[:, 2]
        gain = v("gain").rearrange("p (n j) -> p n j", j=KD)
        w_gates = v("w_gates").rearrange("p (k n) -> p k n", n=8)
        rms, inv_rms = mixer[:, 32], mixer[:, 33:34]
        x_view = x_t.rearrange("(j p) t -> p j t", p=P)
        out_view = out_t.rearrange("(j p) t -> p j t", p=P)

        def mod_part(layer, part):
            c = (layer * 6 + part) * KD
            return mod[:, c:c + KD]

        def tiles(a, b):
            return mixer[:, a:b, :]

        def flat(a, b):
            return mixer[:, a:b, :].rearrange("p a t -> p (a t)")

        V_A = 16
        def probs(h):
            return flat(56 + 2 * (h % 2), 58 + 2 * (h % 2))[:, 0:384]

        def bias(h):
            return flat(60 + 2 * (h % 2), 62 + 2 * (h % 2))[:, 0:384]

        def probs_t(h):
            return flat(84 + 2 * (h % 2), 86 + 2 * (h % 2))[:, 0:384]

        v_rows = mixer[:, 48:56, :].rearrange("p (s a) t -> p s (a t)", s=2)
        taps = v("ab_conv").rearrange("p (g k) -> p g k", k=3)

        Q_D, K_D, V_D, G_RG, OG = 8, 16, 24, 32, 40
        rg_blocks = flat(56, 64).rearrange("p (n g j) -> p n g j", n=2, g=8)
        rtaps = v("rg_conv").rearrange("p (g k) -> p g k", k=4)

        def row(n):
            return summed[0:4, n, :]

        def decay(h):
            return flat(56 + 2 * (h % 2), 58 + 2 * (h % 2))[:, 0:384]

        def den(h):
            return mixer[:, 60 + h % 2, :]

        def weighted(h):
            return flat(K_D + 2 * h, K_D + 2 * h + 2)[:, 0:384]

        def y_pair(gm, j):
            at = (2 * j if j < 4 else 72 + 2 * (j - 4)) if gm is ab_out else (64 + 2 * j if j < 4 else Q_D + 2 * (j - 4))
            return tiles(at, at + 2)

        norms = {ab: (0, 0, 0), up0: (1, 0, 3), cd: (2, 1, 0), up1: (3, 1, 3)}
        final_norm = 4

        def chunk_low(gm, i, half, j):
            jj = j + gm.offset(half)
            q = gm.quads(i, half) + jj // RING
            if jj % RING == RING - 1:
                return low_ready_pool, q + 1
            return low_ready, q * (RING - 1) + jj % RING + 1

        RESIDUALS = {ab_out: 0, down0: 1, cd_out: 2, down1: 3}

        def residual_tile(gm, i, half, f):
            return RESIDUALS[gm] * KD + i * 8 + half * GROUP + f

        def prefilled(gm):
            return gm in norms

        def idle(half, n):
            return bank[4 * (1 - half) + n]

        def head_bank(h, n):
            half, first = ((1, 0), (0, 0), (0, 2), (1, 0))[h]
            return idle(half, first + n)

        block = ctx.enter_context(nc.Block())

        @block.sync
        def _(sp):
            def load_raw(gm, i, half, j):
                jj = j + gm.offset(half)
                g = gm.quads(i, half) * RING + jj
                s, count = chunk_low(gm, i, half, j)
                wait(sp, s, count - (1 if s is low_ready_pool else RING - 1))
                sp.dma_start(raw[:, jj % RING], weights[bass.ds(g, 1)].rearrange(
                    "g p (k n) -> p (g k) n", k=CHUNK_K)).then_inc(raw_landed[jj % RING], 16)

            def load_mod(group, j):
                g = group * MOD_CHUNKS + j
                wait(sp, mod_added, g - RING + 1)
                sp.dma_start(mod_raw[:, j % RING], mod_weights[bass.ds(g, 1)].rearrange(
                    "g p (k n) -> p (g k) n", k=CHUNK_K)).then_inc(mod_landed[j % RING], 16)

            sp.dma_start(vec[:], vectors).then_inc(vectors_landed, 16)
            for j in range(MOD_CHUNKS):
                load_mod(0, j)
            sp.dma_start(tab[:], tables).then_inc(tables_landed, 16)
            sp.dma_start(gate_flat[:, 0:384], distances).then_inc(tables_landed, 16)
            sp.dma_start(gbias[:], gate_b).then_inc(tables_landed, 16)
            sp.dma_start(x[:], x_view).then_inc(x_landed, 16)
            with sp.Fori(1, 8) as i:
                for j in range(MOD_CHUNKS):
                    load_mod(i, j)

            def body(gm, i):
                for half in range(2):
                    for j in range(gm.n):
                        load_raw(gm, i, half, j)
                        if gm is cd and (i, half, j) == (0, 0, 3):
                            sp.wait_ge(tile_out, gm.tile0)
                            sp.wait_ge(square_sum, 3)
                            sp.dma_start(flat(56, 64), rg_w).then_inc(rg_landed, 16)
                            sp.dma_start(gate_flat[:, 0:896], futures).then_inc(futures_landed, 16)
                        m = gm.mod_chunk(i, half, j)
                        if m:
                            load_mod(gm.groups(i, half) + m[0], m[1])

            for gm in gemms:
                for part in gm.parts():
                    if isinstance(part, int):
                        body(gm, part)
                    else:
                        with sp.Fori(*part) as i:
                            body(gm, i)

            for q in range(4):
                sp.wait_ge(normalised, 4 * (q + 1))
                sp.dma_start(out_view[:, 4 * q:4 * q + 4], tiles(4 * q, 4 * q + 4)).then_inc(out_landed, 16)
            sp.wait_ge(out_landed, 64)

        @block.gpsimd
        def _(pool):
            def body(gm, i):
                for half in range(2):
                    for j in range(gm.n):
                        jj = j + gm.offset(half)
                        if jj % RING == RING - 1:
                            pool.wait_ge(high_ready, gm.quads(i, half) * RING + jj + 1)
                            nc.gpsimd.tensor_tensor(low[:, RING - 1], raw[:, RING - 1],
                                                    high[:, RING - 1].bitcast(F32),
                                                    ALU.subtract).then_inc(low_ready_pool, 1)

            for gm in gemms:
                for part in gm.parts():
                    if isinstance(part, int):
                        body(gm, part)
                    else:
                        with pool.Fori(*part) as i:
                            body(gm, i)

        @block.scalar
        def _(act):
            steps = [0]

            def link(ins):
                steps[0] += 1
                ins.then_inc(act_step, 1)
                act.wait_ge(act_step, steps[0])

            def split_high(gm, i, half, j):
                jj = j + gm.offset(half)
                q = gm.quads(i, half)
                act.wait_ge(raw_landed[jj % RING], q * 16 + 16 * (jj // RING + 1))
                wait(act, chunk_used, q * RING + jj - RING + 1)
                nc.scalar.activation(high[:, jj % RING], raw[:, jj % RING], ACT.Copy).then_inc(high_ready, 1)

            def copy_cross(gm, i, half, f):
                wait(act, tile_out, gm.tiles(i, half) + f - GROUP + 1)
                nc.scalar.copy(cross[:, f], bank[4 * half + f][:, T:2 * T]).then_inc(cross_copied, 1)

            def after_tile(gm, i, half, f):
                if gm.kind == "swiglu" and half == 0:
                    act.wait_ge(tile_out, gm.tiles(i, 0) + f + 1)
                    nc.scalar.activation(gate[:, f], gate[:, f], ACT.Silu).then_inc(gate_ready, 1)
                elif gm.kind == "swiglu":
                    h0 = 0 if gm is up0 else KF
                    act.wait_ge(hidden_ready, h0 + i * GROUP + f + 1)
                    nc.scalar.activation(hidden[:, bass.ds(i * GROUP + f, 1), 0], summed[:, f:f + 1],
                                         ACT.Copy).then_inc(hidden_high, 1)
                elif gm.kind == "residual":
                    n = residual_tile(gm, i, half, f)
                    act.wait_ge(x_updated, n + 1)
                    wait(act, squares_added, n - 1)
                    nc.scalar.activation(square[:, n % 2], x[:, n % KD], ACT.Square).then_inc(x_squared, 1)

            def body(gm, i):
                for half in range(2):
                    before, _ = gm.previous(i, half)
                    first = isinstance(i, int) and (i, half) == (0, 0)
                    for j in range(gm.n):
                        if first and gm.fed is not None and j >= RING:
                            feed(gm, j)
                        if not (first and j < RING and prefilled(gm)):
                            split_high(gm, i, half, j)
                        if before and 2 <= j < 2 + GROUP:
                            if j == 2:
                                act.wait_ge(chunk_used, gm.quads(i, half) * RING + gm.offset(half))
                            copy_cross(*before, j - 2)
                        if before and 3 <= j < 3 + GROUP:
                            after_tile(*before, j - 3)
                        if gm in (ab, cd) and isinstance(i, int):
                            mixer_step(gm, 2 * i + half, half, j)
                        if gm is cd_out and first and j == 5:
                            act.wait_ge(tile_out, cd_out.tile0)
                            nc.scalar.activation(tiles(OG + 4, OG + 8), tiles(OG + 4, OG + 8),
                                                 ACT.Sigmoid).then_inc(og_ready, 1)

            def gemm(gm):
                if prefilled(gm):
                    for j in range(RING):
                        split_high(gm, 0, 0, j)
                if gm in norms:
                    norm(norms[gm][0])
                if gm.fed is not None:
                    if gm.before is not None:
                        act.wait_ge(chunk_used, gm.quad0 * RING)
                    for j in range(RING):
                        feed(gm, j)
                for part in gm.parts():
                    if isinstance(part, int):
                        body(gm, part)
                    else:
                        with act.Fori(*part) as i:
                            body(gm, i)

            def drain(gm):
                last = gm.bodies - 1
                nc.scalar.activation(small[:, 96:97], small[:, 95:96], ACT.Sqrt)
                act.wait_ge(chunk_used, (gm.quad0 + gm.bodies * gm.n // 2) * RING)
                for f in range(GROUP):
                    copy_cross(gm, last, 1, f)
                    if f:
                        after_tile(gm, last, 1, f - 1)
                after_tile(gm, last, 1, GROUP - 1)

            def norm(n):
                act.wait_ge(square_sum, n + 1)
                nc.scalar.activation(rms, bank[0][:, 0:T], ACT.Sqrt, bias=small[:, 95:96],
                                     scale=1.0 / D).then_inc(rms_ready, 1)

            def feed(gm, j):
                if gm in norms:
                    n, layer, part = norms[gm]
                    shift = mod_part(layer, part)
                    act.wait_ge(normed_ready, n * 8 + j + 1)
                    for k in (2 * j, 2 * j + 1):
                        ins = nc.scalar.activation(acts[:, k, 0], mixer[:, k], ACT.Identity, bias=shift[:, k:k + 1])
                else:
                    if j >= 4:
                        act.wait_ge(*((conv_ready, 1 if j < 6 else 2) if gm is ab_out
                                      else (mlstm_y_ready, 1 if j < 6 else 2)))
                    else:
                        act.wait_ge(*((heads_stored, 2 * j + 2) if gm is ab_out else (rg_y_ready, 1)))
                    ins = nc.scalar.activation(acts[:, 2 * j:2 * j + 2, 0], y_pair(gm, j), ACT.Copy)
                ins.then_inc(feed_high, 1)

            def copy_values(b, half, n):
                act.wait_ge(v_turned, b + 1)
                q = b % 4
                nc.scalar.copy(v_rows[:, q // 2, 512 * (q % 2):512 * (q % 2) + 512],
                               idle(half, n)[:]).then_inc(v_stored, 1)

            def mixer_step(gm, n, half, j):
                if gm is ab:
                    attention_step(n, half, j)
                else:
                    layer1_step(n, half, j)

            def attention_step(n, half, j):
                if n == 6 and j == 7:
                    for b in range(2):
                        copy_values(b, half, b)
                if n == 7 and j == 1:
                    for b in range(2):
                        copy_values(2 + b, 1 - half, b)
                if 7 <= n <= 10 and j == 7:
                    for h in (2 * (n - 7), 2 * (n - 7) + 1):
                        act.wait_ge(probs_turned, h + 1)
                        wait(act, heads_out, h - 1)
                        nc.scalar.copy(probs_t(h), idle(half, h % 2)[:, 0:384]).then_inc(probs_stored, 1)
                if 6 <= n <= 9 and j == 6:
                    act.wait_ge(tables_landed, 48)
                    for h in (2 * (n - 6), 2 * (n - 6) + 1):
                        wait(act, scores_max, h - 1)
                        nc.scalar.mul(bias(h), distance, 2.0 ** (-8.0 * (h + 1) / HEADS_A)).then_inc(bias_ready, 1)
                if 6 <= n <= 9 and j == 7:
                    for h in (2 * (n - 6), 2 * (n - 6) + 1):
                        act.wait_ge(scores_max, h + 1)
                        for q, (a, b) in enumerate(((0, 128), (128, 384))):
                            c = 2 * h + q
                            nc.scalar.activation(probs(h)[:, a:b], probs(h)[:, a:b], ACT.Exp, bias=small[:, c:c + 1],
                                                 accum_out=small[:, 16 + c:17 + c]).then_inc(probs_exp, 1)
                if 8 <= n <= 11 and j == 1:
                    for h in (2 * (n - 8), 2 * (n - 8) + 1):
                        act.wait_ge(heads_out, h + 1)
                        nc.scalar.copy(mixer[:, h], idle(1 - half, h % 2)[:, 0:T]).then_inc(heads_stored, 1)

            def rg_gates(gs, half):
                for g, b in gs:
                    act.wait_ge(rg_products, g + 1)
                    for q, (name, at) in enumerate((("rg_ba", 72), ("rg_bx", 80))):
                        nc.scalar.activation(mixer[:, at + g], idle(half, b)[:, q * T:q * T + T], ACT.Sigmoid,
                                             bias=v(name)[:, g:g + 1]).then_inc(rg_sigmoid, 1)

            def layer1_step(n, half, j):
                if (n, j) == (0, 6):
                    nc.scalar.activation(gates_w[:, :, 0], w_gates, ACT.Copy).then_inc(gates_high, 1)
                if (n, j) == (1, 7):
                    act.wait_ge(gates_done, 1)
                    nc.scalar.copy(small[:, 0:32], idle(half, 0)[:, 0:32]).then_inc(gates_copied, 1)
                if (n, j) == (2, 1):
                    link(nc.scalar.activation(small[:, 40:48], v("rg_lambda"), ACT.Abs))
                    nc.scalar.activation(small[:, 40:48], small[:, 40:48], ACT.Exp, scale=-1.0).then_inc(lam_exp, 1)
                if (n, j) == (2, 3):
                    act.wait_ge(lam_exp1, 1)
                    nc.scalar.activation(small[:, 48:56], small[:, 40:48], ACT.Ln).then_inc(lam_log, 1)
                if (n, j) == (3, 0):
                    act.wait_ge(f_rows, 1)
                    link(nc.scalar.activation(row(2), row(1), ACT.Abs))
                    nc.scalar.activation(row(2), row(2), ACT.Exp, scale=-1.0).then_inc(f_exp, 1)
                if (n, j) == (3, 2):
                    act.wait_ge(f_exp1, 1)
                    nc.scalar.activation(row(2), row(2), ACT.Ln).then_inc(f_log, 1)
                if (n, j) == (3, 6):
                    act.wait_ge(m_rows, 1)
                    nc.scalar.activation(row(3), row(2), ACT.Exp, scale=-1.0).then_inc(m_exp, 1)
                if (n, j) == (4, 7):
                    rg_gates(((0, 0), (1, 1), (2, 2)), half)
                if (n, j) == (5, 7):
                    rg_gates(((3, 0), (4, 1), (5, 2)), half)
                if (n, j) == (6, 2):
                    rg_gates(((6, 0), (7, 1)), 1 - half)
                if n in (6, 7) and j == 7:
                    for h in (2 * (n - 6), 2 * (n - 6) + 1):
                        act.wait_ge(w_minus, h + 1)
                        nc.scalar.activation(decay(h), decay(h), ACT.Exp, scale=-1.0).then_inc(w_exp, 1)
                if (n, j) == (7, 1):
                    act.wait_ge(log_a_ready, 1)
                    link(nc.scalar.activation(tiles(0, 8), tiles(72, 80), ACT.Exp))
                    nc.scalar.activation(tiles(72, 80), tiles(72, 80), ACT.Tanh, scale=-1.0).then_inc(a_ready, 1)
                if (n, j) == (8, 0):
                    act.wait_ge(u_square, 1)
                    nc.scalar.activation(tiles(64, 72), tiles(64, 72), ACT.Sqrt).then_inc(u_root, 1)
                if (n, j) == (8, 7):
                    for b in range(2):
                        copy_values(4 + b, half, b)
                if (n, j) == (9, 1):
                    for b in range(2, 4):
                        copy_values(4 + b, 1 - half, b)
                for h in {9: (0,), 10: (1, 2), 11: (3,)}.get(n, ()) if j == 7 else ():
                    act.wait_ge(num_ready, h + 1)
                    wait(act, head_done, h - 1)
                    nc.scalar.activation(den(h), head_bank(h, 0)[:, 0:T], ACT.Abs).then_inc(den_abs, 1)
                if (n, j) == (10, 6):
                    act.wait_ge(tile_out, cd.tiles(5, 0))
                    nc.scalar.activation(tiles(G_RG, G_RG + 8), tiles(G_RG, G_RG + 8),
                                         ACT.Gelu_apprx_tanh).then_inc(gelu_ready, 1)
                if (n, j) == (11, 6):
                    act.wait_ge(tile_out, cd.tiles(5, 1))
                    nc.scalar.activation(tiles(OG, OG + 4), tiles(OG, OG + 4), ACT.Sigmoid).then_inc(og_ready, 1)

            act.wait_ge(vectors_landed, 16)
            nc.scalar.activation(cond[:], v("cond"), ACT.Silu).then_inc(cond_ready, 1)
            act.wait_ge(x_landed, 16)
            for j in range(4):
                nc.scalar.activation(tiles(16 + 4 * j, 20 + 4 * j), x[:, 4 * j:4 * j + 4],
                                     ACT.Square).then_inc(x_squared, 1)
            act.wait_ge(dve_step, 1)

            gemm(ab)
            gemm(ab_out)
            drain(ab_out)
            gemm(up0)
            gemm(down0)
            drain(down0)
            gemm(cd)
            gemm(cd_out)
            drain(cd_out)
            gemm(up1)
            gemm(down1)
            drain(down1)
            norm(final_norm)

        @block.vector
        def _(dve):
            steps = [0]

            def link(ins):
                steps[0] += 1
                ins.then_inc(dve_step, 1)
                dve.wait_ge(dve_step, steps[0])

            def split_low(gm, i, half, j):
                jj = j + gm.offset(half)
                s = jj % RING
                if s == RING - 1:
                    return
                dve.wait_ge(high_ready, gm.quads(i, half) * RING + jj + 1)
                nc.vector.tensor_tensor(low[:, s], raw[:, s], high[:, s].bitcast(F32),
                                        ALU.subtract).then_inc(low_ready, 1)

            def add_mod(group, j, acc=mod_acc):
                s = j % RING
                dve.wait_ge(mod_landed[s], group * 32 + 16 * (j // RING + 1))
                for k in range(CHUNK_K):
                    w, cs = mod_raw[:, s, k], cond[:, 2 * j + k:2 * j + k + 1]
                    a = acc[:, k * 2:k * 2 + 2].rearrange("p a t -> p (a t)") if acc is cross else acc[:, k]
                    if j == 0:
                        ins = nc.vector.tensor_scalar(a, w, cs, None, ALU.mult)
                    else:
                        if k == 0:
                            dve.wait_ge(mod_added, group * MOD_CHUNKS + j)
                        ins = nc.vector.scalar_tensor_tensor(a, w, cs, a, ALU.mult, ALU.add)
                ins.then_inc(mod_added, 1)

            def store_mod(group, b):
                dve.wait_ge(mod_reduced, group + 1)
                nc.vector.tensor_tensor(mod[:, bass.ds(group * 4, 4)], b[:, 0:4],
                                        v("mod_b")[:, bass.ds(group * 4, 4)], ALU.add).then_inc(mod_ready, 1)

            def tile_done(gm, i, half, f):
                tile = gm.tiles(i, half) + f
                dve.wait_ge(cross_copied, tile + 1)
                main = bank[4 * half + f][:, 0:T]
                if gm.kind == "store":
                    nc.vector.tensor_tensor(mixer[:, bass.ds(i * 8 + 4 * half + f, 1)],
                                            cross[:, f:f + 1], main.rearrange("p (a t) -> p a t", a=1),
                                            ALU.add).then_inc(tile_out, 1)
                elif gm.kind == "residual":
                    layer = 0 if gm in (ab_out, down0) else 1
                    gates = mod_part(layer, 2 if gm in (ab_out, cd_out) else 5)
                    nc.vector.tensor_tensor(summed[:, f], cross[:, f], main, ALU.add).then_inc(tile_out, 1)
                    dve.wait_ge(tile_out, tile + 1)
                    n = i * 8 + 4 * half + f
                    nc.vector.scalar_tensor_tensor(x[:, n], summed[:, f], gates[:, n:n + 1], x[:, n],
                                                   ALU.mult, ALU.add).then_inc(x_updated, 1)
                elif half == 0:
                    nc.vector.tensor_tensor(gate[:, f], cross[:, f], main, ALU.add).then_inc(tile_out, 1)
                else:
                    h0 = 0 if gm is up0 else KF
                    wait(dve, hidden_high, h0 + (i - 1) * GROUP + f + 1)
                    nc.vector.tensor_tensor(summed[:, f], cross[:, f], main, ALU.add).then_inc(tile_out, 1)
                    dve.wait_ge(tile_out, tile + 1)
                    dve.wait_ge(gate_ready, h0 + i * GROUP + f + 1)
                    nc.vector.tensor_tensor(summed[:, f], summed[:, f], gate[:, f],
                                            ALU.mult).then_inc(hidden_ready, 1)

            def after_tile(gm, i, half, f):
                if gm.kind == "swiglu" and half == 1:
                    h0 = 0 if gm is up0 else KF
                    dve.wait_ge(hidden_high, h0 + i * GROUP + f + 1)
                    n = i * GROUP + f
                    nc.vector.tensor_tensor(hidden[:, bass.ds(n, 1), 1], summed[:, f:f + 1],
                                            hidden[:, bass.ds(n, 1), 0].bitcast(F32),
                                            ALU.subtract).then_inc(hidden_low, 1)
                if gm.kind == "residual":
                    n = residual_tile(gm, i, half, f)
                    dve.wait_ge(x_squared, 4 + n + 1)
                    if n % KD == 0:
                        ins = nc.vector.tensor_copy(square_acc, square[:, n % 2])
                    else:
                        dve.wait_ge(squares_added, n)
                        ins = nc.vector.tensor_tensor(square_acc, square_acc, square[:, n % 2], ALU.add)
                    ins.then_inc(squares_added, 1)

            def body(gm, i):
                for half in range(2):
                    groups = gm.groups(i, half)
                    before, carried = gm.previous(i, half)
                    first = isinstance(i, int) and (i, half) == (0, 0)
                    for j in range(gm.n):
                        if first and gm.fed is not None and j >= RING:
                            feed(gm, j)
                        if not (first and j < RING and prefilled(gm)):
                            split_low(gm, i, half, j)
                        if j == 2 and carried:
                            store_mod(groups - 1, idle(1 - half, 3))
                        if j == 12 and gm.m(i) == 4:
                            store_mod(groups, idle(half, 3))
                        if before and 2 <= j < 2 + GROUP:
                            tile_done(*before, j - 2)
                        if before and 4 <= j < 4 + GROUP:
                            after_tile(*before, j - 4)
                        m = gm.mod_chunk(i, half, j)
                        if m:
                            if m[1] == 0:
                                dve.wait_ge(mod_reduced, groups + m[0])
                            add_mod(groups + m[0], m[1])
                        if gm in (ab, cd) and isinstance(i, int):
                            mixer_step(gm, 2 * i + half, half, j)
                        if first and gm is ab_out and j == 5:
                            dve.wait_ge(tile_out, ab_out.tile0)
                            link(nc.vector.tensor_tensor(tiles(76, 80), tiles(76, 80), tiles(44, 48), ALU.mult))
                            nc.vector.tensor_copy(small[:, 94:95], small[:, 95:96]).then_inc(conv_ready, 1)
                        if first and gm is cd_out and j == 5:
                            gate_heads(1)

            def gemm(gm):
                if prefilled(gm):
                    for j in range(RING):
                        split_low(gm, 0, 0, j)
                if gm in norms:
                    norm(gm)
                if gm.fed is not None:
                    for j in range(RING):
                        feed(gm, j)
                for part in gm.parts():
                    if isinstance(part, int):
                        body(gm, part)
                    else:
                        with dve.Fori(*part) as i:
                            body(gm, i)

            def drain(gm):
                last = gm.bodies - 1
                if gm.carries(last, 1):
                    store_mod(gm.groups(last, 1) + max(1, gm.m(last) // 2) - 1, bank[3])
                for f in range(GROUP):
                    tile_done(gm, last, 1, f)
                    if f:
                        after_tile(gm, last, 1, f - 1)
                after_tile(gm, last, 1, GROUP - 1)

            def inverse(n):
                dve.wait_ge(rms_ready, n + 1)
                link(nc.vector.reciprocal(inv_rms[:, 0], rms))

            def norm(gm):
                n, layer, part = norms[gm]
                dve.wait_ge(mod_ready, (layer * 6 + part + 2) * 4)
                link(nc.vector.scalar_tensor_tensor(norm_gain[:], mod_part(layer, part + 1), 1.0,
                                                    gain[:, n], ALU.add, ALU.mult))
                inverse(n)
                normed(gm, 0)

            def normed(gm, j):
                for k in (2 * j, 2 * j + 1):
                    ins = nc.vector.scalar_tensor_tensor(mixer[:, k], x[:, k], norm_gain[:, k:k + 1], inv_rms[:, 0],
                                                         ALU.mult, ALU.mult)
                ins.then_inc(normed_ready, 1)

            def feed(gm, j):
                if gm in norms:
                    n, layer, part = norms[gm]
                    shift = mod_part(layer, part)
                    if j < 7:
                        normed(gm, j + 1)
                    dve.wait_ge(feed_high, 8 * gm.fed + j + 1)
                    for k in (2 * j, 2 * j + 1):
                        ins = nc.vector.scalar_tensor_tensor(acts[:, k, 1], mixer[:, k], shift[:, k:k + 1],
                                                             acts[:, k, 0].bitcast(F32), ALU.add, ALU.subtract)
                else:
                    dve.wait_ge(feed_high, 8 * gm.fed + j + 1)
                    ins = nc.vector.tensor_tensor(acts[:, 2 * j:2 * j + 2, 1], y_pair(gm, j),
                                                  acts[:, 2 * j:2 * j + 2, 0].bitcast(F32), ALU.subtract)
                ins.then_inc(feed_low, 1)

            def mixer_step(gm, n, half, j):
                if gm is ab:
                    attention_step(n, half, j)
                    conv_step(n, j)
                else:
                    layer1_step(n, half, j)

            def attention_step(n, half, j):
                if 6 <= n <= 9 and j == 7:
                    pair = (2 * (n - 6), 2 * (n - 6) + 1)
                    for h in pair:
                        p = probs(h)
                        dve.wait_ge(scores_ready, h + 1)
                        dve.wait_ge(bias_ready, h + 1)
                        wait(dve, probs_turned, h - 1)
                        link(nc.vector.scalar_tensor_tensor(p, idle(half, 2 + h % 2)[:, 0:384], float(P) ** -0.5,
                                                            bias(h), ALU.mult, ALU.add))
                        link(nc.vector.reduce_max(small[:, 2 * h:2 * h + 1], p[:, 0:128], AX.X, negate=True))
                        nc.vector.reduce_max(small[:, 2 * h + 1:2 * h + 2], p[:, 128:384], AX.X,
                                             negate=True).then_inc(scores_max, 1)
                    for h in pair:
                        p = probs(h)
                        dve.wait_ge(probs_exp, 2 * h + 2)
                        link(nc.vector.reciprocal(small[:, 32 + 2 * h:34 + 2 * h], small[:, 16 + 2 * h:18 + 2 * h]))
                        link(nc.vector.tensor_scalar(p[:, 0:128], p[:, 0:128], small[:, 32 + 2 * h:33 + 2 * h],
                                                     None, ALU.mult))
                        nc.vector.tensor_scalar(p[:, 128:384], p[:, 128:384], small[:, 33 + 2 * h:34 + 2 * h],
                                                None, ALU.mult).then_inc(probs_ready, 1)

            def conv_tile(g):
                u, y = mixer[:, 64 + g], mixer[:, 72 + g]
                link(nc.vector.tensor_scalar(y, u, taps[:, g, 2:3], None, ALU.mult))
                link(nc.vector.scalar_tensor_tensor(y[:, 1:T], u[:, 0:T - 1], taps[:, g, 1:2], y[:, 1:T],
                                                    ALU.mult, ALU.add))
                link(nc.vector.scalar_tensor_tensor(y[:, 2:T], u[:, 0:T - 2], taps[:, g, 0:1], y[:, 2:T],
                                                    ALU.mult, ALU.add))

            def conv_step(n, j):
                if (n, j) == (8, 6):
                    dve.wait_ge(tile_out, ab.tiles(4, 0))
                    link(nc.vector.tensor_tensor(tiles(64, 68), tiles(24, 28), tiles(28, 32), ALU.mult))
                if n == 9 and j < 4:
                    conv_tile(j)
                if (n, j) == (10, 6):
                    dve.wait_ge(tile_out, ab.tiles(4, 1))
                    nc.vector.tensor_tensor(tiles(72, 76), tiles(72, 76), tiles(32, 36), ALU.mult).then_inc(conv_ready, 1)
                if (n, j) == (11, 6):
                    dve.wait_ge(tile_out, ab.tiles(5, 1))
                    link(nc.vector.tensor_tensor(tiles(68, 72), tiles(36, 40), tiles(40, 44), ALU.mult))
                if n == 11 and j >= 6:
                    conv_tile(4 + 2 * (j - 6))
                    conv_tile(5 + 2 * (j - 6))

            def rg_conv_tile(g):
                u, y = mixer[:, g], mixer[:, 64 + g]
                link(nc.vector.tensor_scalar(y, u, rtaps[:, g, 3:4], v("rg_conv_b")[:, g:g + 1], ALU.mult, ALU.add))
                for k in range(2, -1, -1):
                    s = 3 - k
                    ins = nc.vector.scalar_tensor_tensor(y[:, s:T], u[:, 0:T - s], rtaps[:, g, k:k + 1], y[:, s:T],
                                                         ALU.mult, ALU.add)
                    if k:
                        link(ins)
                    else:
                        ins.then_inc(rg_conv_ready, 1)

            def gate_heads(q):
                dve.wait_ge(og_ready, q + 1)
                dve.wait_ge(head_done, 2 * q + 2)
                y = tiles(Q_D + 4 * q, Q_D + 4 * q + 4)
                nc.vector.tensor_tensor(y, y, tiles(OG + 4 * q, OG + 4 * q + 4), ALU.mult).then_inc(mlstm_y_ready, 1)

            def layer1_step(n, half, j):
                if (n, j) == (0, 7):
                    dve.wait_ge(gates_high, 1)
                    nc.vector.tensor_tensor(gates_w[:, :, 1], w_gates, gates_w[:, :, 0].bitcast(F32),
                                            ALU.subtract).then_inc(gates_split, 1)
                if (n, j) == (2, 0):
                    dve.wait_ge(gates_copied, 1)
                    g4 = small[:, 0:32].rearrange("p (s b n) -> p s b n", s=2, b=2)
                    nc.vector.tensor_tensor(small[:, 64:80].rearrange("p (s n) -> p s n", s=2), g4[:, :, 0],
                                            g4[:, :, 1], ALU.add).then_inc(gates_summed, 1)
                if (n, j) == (2, 2):
                    dve.wait_ge(lam_exp, 1)
                    nc.vector.tensor_scalar(small[:, 40:48], small[:, 40:48], 1.0, None, ALU.add).then_inc(lam_exp1, 1)
                if (n, j) == (2, 4):
                    link(nc.vector.tensor_scalar(small[:, 32:40], v("rg_lambda"), -1.0, 0.0, ALU.mult, ALU.max))
                    dve.wait_ge(lam_log, 1)
                    link(nc.vector.tensor_tensor(small[:, 32:40], small[:, 32:40], small[:, 48:56], ALU.add))
                    link(nc.vector.tensor_scalar(small[:, 32:40], small[:, 32:40], -8.0, None, ALU.mult))
                if (n, j) == (2, 7):
                    dve.wait_ge(gates_rows, 1)
                    link(nc.vector.tensor_scalar(row(0), idle(half, 0)[0:4, 0:T], gbias[0:4, 0:1], None, ALU.add))
                    nc.vector.tensor_scalar(row(1), idle(half, 0)[0:4, T:2 * T], gbias[0:4, 1:2], None,
                                            ALU.add).then_inc(f_rows, 1)
                if (n, j) == (3, 1):
                    dve.wait_ge(f_exp, 1)
                    nc.vector.tensor_scalar(row(2), row(2), 1.0, None, ALU.add).then_inc(f_exp1, 1)
                if (n, j) == (3, 3):
                    dve.wait_ge(f_log, 1)
                    link(nc.vector.scalar_tensor_tensor(row(1), row(1), 0.0, row(2), ALU.min, ALU.subtract))
                    link(nc.vector.tensor_tensor_scan(row(3), t("ones")[0:4], row(1), 0.0, ALU.mult, ALU.add))
                    link(nc.vector.tensor_tensor(row(0), row(0), row(3), ALU.subtract))
                    link(nc.vector.tensor_tensor_scan(row(1), row(0), row(0), 0.0, ALU.max, ALU.max))
                    nc.vector.tensor_tensor(row(2), row(3), row(1), ALU.add).then_inc(m_rows, 1)
                if n == 2 and j >= 6:
                    dve.wait_ge(tile_out, cd.tiles(1, 0))
                    rg_conv_tile(j - 6)
                if n == 3 and j % 2 == 0:
                    rg_conv_tile(2 + j // 2)
                if n == 4 and j < 2:
                    rg_conv_tile(6 + j)
                if (n, j) == (5, 1):
                    dve.wait_ge(a_turned, 1)
                    nc.vector.tensor_copy(small[:, 80:88], idle(1 - half, 3)[:, 0:8]).then_inc(a_stored, 1)
                if (n, j) == (6, 4):
                    dve.wait_ge(rg_sigmoid, 16)
                    for g in range(8):
                        ins = nc.vector.tensor_scalar(mixer[:, 72 + g], mixer[:, 72 + g], small[:, 32 + g:33 + g],
                                                      None, ALU.mult)
                    ins.then_inc(log_a_ready, 1)
                    link(nc.vector.tensor_tensor(tiles(80, 88), tiles(80, 88), tiles(64, 72), ALU.mult))
                if n in (6, 7) and j == 7:
                    pair = (2 * (n - 6), 2 * (n - 6) + 1)
                    dve.wait_ge(futures_landed, 16)
                    dve.wait_ge(a_stored, 1)
                    spread = idle(half, 0)
                    for q, h in enumerate(pair):
                        dve.wait_ge(m_spread, h // 2 + 1)
                        wait(dve, p_ready, h - 1)
                        for s, (a, b) in enumerate(((0, 256), (256, 384))):
                            ins = nc.vector.scalar_tensor_tensor(
                                decay(h)[:, a:b], spread[:, q * T + s * P:q * T + T],
                                small[:, 80 + 4 * s + h:81 + 4 * s + h], future[:, a:b], ALU.subtract, ALU.add)
                        ins.then_inc(w_minus, 1)
                    for q, h in enumerate(pair):
                        dve.wait_ge(w_exp, h + 1)
                        dve.wait_ge(qk_ready, h + 1)
                        nc.vector.scalar_tensor_tensor(weighted(h), idle(half, 1 + q)[:, 0:384], 1.0 / 16.0, decay(h),
                                                       ALU.mult, ALU.mult).then_inc(p_ready, 1)
                if (n, j) == (7, 3):
                    dve.wait_ge(a_ready, 1)
                    link(nc.vector.tensor_tensor(tiles(64, 72), tiles(0, 8), tiles(0, 8), ALU.mult))
                    nc.vector.scalar_tensor_tensor(flat(64, 72), flat(64, 72), 1.0, flat(72, 80), ALU.add,
                                                   ALU.mult).then_inc(u_square, 1)
                if (n, j) == (8, 1):
                    dve.wait_ge(u_root, 1)
                    link(nc.vector.tensor_tensor(tiles(64, 72), tiles(64, 72), tiles(80, 88), ALU.mult))
                if n == 8 and 2 <= j < 6:
                    for g in (2 * (j - 2), 2 * (j - 2) + 1):
                        link(nc.vector.tensor_tensor_scan(mixer[:, 72 + g], mixer[:, g], mixer[:, 64 + g], 0.0,
                                                          ALU.mult, ALU.add))
                for h in {9: (0,), 10: (1, 2), 11: (3,)}.get(n, ()) if j == 7 else ():
                    dve.wait_ge(den_abs, h + 1)
                    link(nc.vector.tensor_tensor(den(h), den(h), head_bank(h, 0)[:, T:2 * T], ALU.max))
                    link(nc.vector.reciprocal(den(h), den(h)))
                    for e in range(TILES_D):
                        ins = nc.vector.tensor_tensor(mixer[:, Q_D + 2 * h + e],
                                                      head_bank(h, 1)[:, e * T:e * T + T], den(h), ALU.mult)
                    ins.then_inc(head_done, 1)
                if (n, j) == (11, 0):
                    dve.wait_ge(gelu_ready, 1)
                    nc.vector.tensor_tensor(tiles(64, 72), tiles(72, 80), tiles(G_RG, G_RG + 8),
                                            ALU.mult).then_inc(rg_y_ready, 1)
                if (n, j) == (11, 7):
                    gate_heads(0)

            link(nc.vector.memset(small[:, 95:96], EPS))
            dve.wait_ge(vectors_landed, 16)
            dve.wait_ge(cond_ready, 1)
            for j in range(MOD_CHUNKS):
                add_mod(0, j)
            for j in range(MOD_CHUNKS):
                add_mod(1, j, cross)
            with dve.Fori(1, 4) as i:
                store_mod(i * 2 - 2, bank[3])
                for j in range(MOD_CHUNKS):
                    add_mod(i * 2, j)
                store_mod(i * 2 - 1, bank[7])
                for j in range(MOD_CHUNKS):
                    add_mod(i * 2 + 1, j, cross)
            store_mod(6, bank[3])
            store_mod(7, bank[7])

            gemm(ab)
            gemm(ab_out)
            drain(ab_out)
            gemm(up0)
            gemm(down0)
            drain(down0)
            gemm(cd)
            gemm(cd_out)
            drain(cd_out)
            gemm(up1)
            gemm(down1)
            drain(down1)
            inverse(final_norm)
            for k in range(KD):
                nc.vector.scalar_tensor_tensor(mixer[:, k], x[:, k], gain[:, final_norm, k:k + 1], inv_rms[:, 0],
                                               ALU.mult, ALU.mult).then_inc(normalised, 1)

        @block.tensor
        def _(pe):
            def sum_mod(group, b, acc=mod_acc):
                pe.wait_ge(mod_added, (group + 1) * MOD_CHUNKS)
                for f in range(4):
                    for k in range(CHUNK_K):
                        a = acc[:, k * 2:k * 2 + 2].rearrange("p a t -> p (a t)") if acc is cross else acc[:, k]
                        ins = pe.matmul(b[:, f:f + 1], a[:, f * P:f * P + P], ones[:, 0:1],
                                        start=(k == 0), stop=(k == CHUNK_K - 1))
                ins.then_inc(mod_reduced, 1)

            def body(gm, i):
                operand = hidden if gm in (down0, down1) else acts
                for half in range(2):
                    groups = gm.groups(i, half)
                    first = isinstance(i, int) and (i, half) == (0, 0)
                    if gm in (ab, cd) and isinstance(i, int):
                        banks_back(gm, 2 * i + half)
                    if first and gm is cd_out:
                        pe.wait_ge(head_done, HEADS_D)
                    for j in range(gm.n):
                        pe.wait_ge(*chunk_low(gm, i, half, j))
                        if first and gm.fed is not None:
                            pe.wait_ge(feed_low, 8 * gm.fed + j + 1)
                        elif first:
                            pe.wait_ge(hidden_low, (0 if gm is down0 else KF) + 2 * j + 2)
                        s = (j + gm.offset(half)) % RING
                        for f in range(GROUP):
                            b = bank[4 * half + f]
                            if j == 0:
                                wait(pe, tile_out, gm.tiles(i, half) + f - 2 * GROUP + 1)
                                if f == GROUP - 1:
                                    pe.wait_ge(mod_ready, groups)
                            for k in range(CHUNK_K):
                                kt = CHUNK_K * j + k
                                wl, wh = low[:, s, k, f * P:f * P + P], high[:, s, k, f * P:f * P + P]
                                last = kt == CHUNK_K * gm.n - 1
                                if last:
                                    pe.matmul(b[:, T:2 * T], wl, operand[:, kt, 0], start=False, stop=False)
                                ins = pe.matmul(b[:], wh, operand[:, kt].rearrange("p a t -> p (a t)"),
                                                start=(kt == 0), stop=last)
                                if not last:
                                    ins = pe.matmul(b[:, T:2 * T], wl, operand[:, kt, 0], start=False, stop=False)
                        ins.then_inc(chunk_used, 1)
                        if gm in (ab, cd) and isinstance(i, int):
                            if j == 3:
                                wait(pe, tile_out, gm.tiles(i, half))
                            mixer_step(gm, 2 * i + half, half, j)
                        r = gm.reduced_after(i, half, j)
                        if r is not None:
                            pe.wait_ge(tile_out, gm.tiles(i, half))
                            sum_mod(groups + r, idle(half, 3))

            def gemm(gm):
                for part in gm.parts():
                    if isinstance(part, int):
                        body(gm, part)
                    else:
                        with pe.Fori(*part) as i:
                            body(gm, i)

            def norm(n):
                pe.wait_ge(squares_added, n * KD)
                pe.matmul(bank[0][:, 0:T], ones, square_acc, start=True, stop=True).then_inc(square_sum, 1)

            def turn_values(first_tile, b, dst):
                for q in range(4):
                    src = mixer[:, first_tile + 4 * (b % 2) + q, P * (b // 2):P * (b // 2) + P]
                    ins = pe.transpose(dst[:, q * P:q * P + P], src, ident)
                ins.then_inc(v_turned, 1)

            def banks_back(gm, n):
                if gm is ab:
                    if n == 7:
                        pe.wait_ge(v_stored, 4)
                    if 7 <= n <= 10:
                        pe.wait_ge(scores_max, 2 * (n - 6))
                    if 8 <= n <= 11:
                        pe.wait_ge(heads_stored, 2 * (n - 7))
                    return
                for s, count in {2: [(gates_copied, 1)], 3: [(f_rows, 1)], 5: [(rg_sigmoid, 6), (a_stored, 1)],
                                 6: [(rg_sigmoid, 16)], 7: [(p_ready, 2)], 8: [(p_ready, 4)], 9: [(v_stored, 8)],
                                 10: [(head_done, 1)], 11: [(head_done, 3)]}.get(n, ()):
                    pe.wait_ge(s, count)

            def mixer_step(gm, n, half, j):
                if gm is ab:
                    attention_step(n, half, j)
                else:
                    layer1_step(n, half, j)

            def attention_step(n, half, j):
                if n == 6 and j in (3, 5):
                    for q in range(2):
                        b = q if j == 3 else 2 + q
                        if j == 5:
                            pe.wait_ge(v_stored, q + 1)
                        turn_values(V_A, b, idle(half, q))
                if 7 <= n <= 10 and j == 3:
                    for h in (2 * (n - 7), 2 * (n - 7) + 1):
                        pe.wait_ge(probs_ready, h + 1)
                        for q in range(3):
                            ins = pe.transpose(idle(half, h % 2)[:, q * P:q * P + P], probs(h)[:, q * P:q * P + P],
                                               ident)
                        ins.then_inc(probs_turned, 1)
                if 6 <= n <= 9 and j == 3:
                    for h in (2 * (n - 6), 2 * (n - 6) + 1):
                        q, k, s = mixer[:, h], mixer[:, 8 + h], idle(half, 2 + h % 2)
                        pe.matmul(s[:, 0:128], q[:, 0:P], k[:, 0:P], start=True, stop=True)
                        pe.matmul(s[:, 128:384], q[:, P:T], k, start=True, stop=True).then_inc(scores_ready, 1)
                if 7 <= n <= 10 and j == 5:
                    for h in (2 * (n - 7), 2 * (n - 7) + 1):
                        pe.wait_ge(probs_stored, h + 1)
                        pe.wait_ge(v_stored, 4)
                        o = idle(half, h % 2)
                        pe.matmul(o[:, 0:T], v_rows[:, 0, h * P:h * P + P], probs_t(h)[:, 0:256],
                                  start=True, stop=False)
                        pe.matmul(o[:, P:T], v_rows[:, 1, h * P:h * P + P], probs_t(h)[:, 256:384],
                                  start=False, stop=True).then_inc(heads_out, 1)
                if n in (7, 9) and j == 6:
                    pe.wait_ge(scores_max, 2 * (n - 6) + 2)

            def rg_gate_products(gs, half):
                for g, b in gs:
                    pe.wait_ge(rg_conv_ready, g + 1)
                    for n in range(2):
                        ins = pe.matmul(idle(half, b)[:, n * T:n * T + T], rg_blocks[:, n, g], mixer[:, 64 + g],
                                        start=True, stop=True)
                    ins.then_inc(rg_products, 1)

            def head_products(h):
                w, c0 = weighted(h), head_bank(h, 0)
                pe.matmul(c0[:, 0:T], ones, w[:, 0:256], start=True, stop=False)
                pe.matmul(c0[:, P:T], ones, w[:, 256:384], start=False, stop=True)
                pe.matmul(c0[:, T:2 * T], select[0:4, h], row(3), start=True, stop=True)
                for e in range(TILES_D):
                    c = (2 * h + e) * P
                    o = head_bank(h, 1)[:, e * T:e * T + T]
                    pe.matmul(o, v_rows[:, 0, c:c + P], w[:, 0:256], start=True, stop=False)
                    ins = pe.matmul(o[:, P:T], v_rows[:, 1, c:c + P], w[:, 256:384], start=False, stop=True)
                ins.then_inc(num_ready, 1)

            def layer1_step(n, half, j):
                if (n, j) == (1, 3):
                    pe.wait_ge(gates_split, 1)
                    for s in range(2):
                        for k in range(KD):
                            gp = idle(half, 0)[:, 16 * s:16 * s + 16]
                            pe.matmul(gp, acts[:, k, 0, s * P:s * P + P],
                                      gates_w[:, k].rearrange("p a n -> p (a n)"), start=(k == 0), stop=False)
                            ins = pe.matmul(gp[:, 0:8], acts[:, k, 1, s * P:s * P + P], gates_w[:, k, 0],
                                            start=False, stop=(k == KD - 1))
                    ins.then_inc(gates_done, 1)
                if (n, j) == (2, 3):
                    pe.wait_ge(gates_summed, 1)
                    for q in range(2):
                        for s in range(2):
                            ins = pe.matmul(idle(half, 0)[0:4, q * T + s * P:q * T + s * P + P],
                                            small[:, 64 + 8 * s + 4 * q:68 + 8 * s + 4 * q], ident,
                                            start=True, stop=True)
                    ins.then_inc(gates_rows, 1)
                if (n, j) == (4, 3):
                    pe.wait_ge(rg_landed, 16)
                    rg_gate_products(((0, 0), (1, 1), (2, 2)), half)
                if (n, j) == (4, 5):
                    pe.wait_ge(m_rows, 1)
                    for s in range(2):
                        ins = pe.matmul(idle(half, 3)[:, 4 * s:4 * s + 4], row(0)[:, s * P:s * P + P],
                                        ident[0:4, 0:4], start=True, stop=True)
                    ins.then_inc(a_turned, 1)
                if (n, j) == (5, 3):
                    rg_gate_products(((3, 0), (4, 1), (5, 2)), half)
                if (n, j) == (5, 6):
                    pe.wait_ge(rg_sigmoid, 10)
                    rg_gate_products(((6, 0), (7, 1)), half)
                if n in (6, 7) and j == 3:
                    pair = (2 * (n - 6), 2 * (n - 6) + 1)
                    pe.wait_ge(futures_landed, 16)
                    for q, h in enumerate(pair):
                        ins = pe.matmul(idle(half, 0)[:, q * T:q * T + T], select[0:4, h], row(1),
                                        start=True, stop=True)
                    ins.then_inc(m_spread, 1)
                    for q, h in enumerate(pair):
                        for a, b, s in ((0, 256, 0), (256, 384, P)):
                            for d in range(TILES_D):
                                qt, kt = mixer[:, Q_D + 2 * h + d], mixer[:, K_D + 2 * h + d]
                                ins = pe.matmul(idle(half, 1 + q)[:, a:b], kt[:, s:s + P], qt[:, s:T],
                                                start=(d == 0), stop=(d == 1))
                        ins.then_inc(qk_ready, 1)
                if n == 8 and j in (3, 5):
                    for b in ((0, 1) if j == 3 else (2, 3)):
                        turn_values(V_D, b, idle(half, b))
                if (n, j) == (9, 3):
                    pe.wait_ge(m_exp, 1)
                    pe.wait_ge(p_ready, HEADS_D)
                    head_products(0)
                if (n, j) == (10, 3):
                    head_products(1)
                if (n, j) == (10, 4):
                    head_products(2)
                if (n, j) == (11, 3):
                    head_products(3)

            pe.wait_ge(tables_landed, 48)
            for j in range(4):
                pe.wait_ge(x_squared, j + 1)
                for q in range(4):
                    k = 4 * j + q
                    ins = pe.matmul(bank[0][:, 0:T], ones, mixer[:, 16 + k], start=(k == 0), stop=(k == KD - 1))
            ins.then_inc(square_sum, 1)
            sum_mod(0, bank[3])
            sum_mod(1, bank[7], cross)
            with pe.Fori(1, 4) as i:
                pe.wait_ge(mod_ready, i * 2 - 1)
                sum_mod(i * 2, bank[3])
                pe.wait_ge(mod_ready, i * 2)
                sum_mod(i * 2 + 1, bank[7], cross)
            gemm(ab)
            gemm(ab_out)
            norm(1)
            gemm(up0)
            gemm(down0)
            norm(2)
            gemm(cd)
            gemm(cd_out)
            norm(3)
            gemm(up1)
            gemm(down1)
            norm(final_norm)


def _chunks(w):
    k, n = w.shape
    return w.reshape(k // 256, 2, 128, n // 512, 512).transpose(3, 0, 2, 1, 4).reshape(n // 512, k // 256, 128, 1024)


AB_ORDER = [0, 1, 2, 3, 4, 5, 8, 10, 6, 9, 11, 7]
CD_ORDER = [0, 1, 4, 5, 6, 7, 8, 9, 2, 3, 10, 11]


def kernel(**inputs):
    import numpy as np
    import concourse.bacc as bacc
    from concourse.bass_utils import run_bass_kernel_spmd

    a = {k: np.asarray(w) for k, w in inputs.items()}

    def columns(vector):
        return vector.reshape(-1, 128).T

    def flat_chunks(w):
        return _chunks(w).reshape(-1, 128, 1024)

    def pairs(w1, w3):
        return np.stack([_chunks(w1), _chunks(w3)], axis=1).reshape(-1, 128, 1024)

    cd_w = a["cd_w_in"][0]
    gates_at = cd_w.shape[1] - 8
    weights = np.concatenate([
        _chunks(a["ab_w_in"][0])[AB_ORDER].reshape(-1, 128, 1024), flat_chunks(a["ab_w_out"][0]),
        pairs(a["ffn_w1"][0], a["ffn_w3"][0]), flat_chunks(a["ffn_w2"][0]),
        _chunks(cd_w[:, :gates_at])[CD_ORDER].reshape(-1, 128, 1024), flat_chunks(a["cd_w_out"][0]),
        pairs(a["ffn_w1"][1], a["ffn_w3"][1]), flat_chunks(a["ffn_w2"][1]),
    ])
    mod_weights = np.concatenate([flat_chunks(a["mod_w"][0]), flat_chunks(a["mod_w"][1])])
    vectors = np.concatenate([
        columns(a["c"][0]), columns(a["mod_b"].reshape(-1)),
        columns(np.concatenate([a["norm_mix_g"][0], a["norm_ffn_g"][0], a["norm_mix_g"][1],
                                a["norm_ffn_g"][1], a["final_norm_g"]])),
        a["ab_conv_w"][0].reshape(3, 8, 128).transpose(2, 1, 0).reshape(128, 24),
        a["rg_conv_w"][0].reshape(4, 8, 128).transpose(2, 1, 0).reshape(128, 32),
        columns(a["rg_conv_b"][0]), columns(a["rg_ba"][0]), columns(a["rg_bx"][0]), columns(a["rg_lambda"][0]),
        cd_w[:, gates_at:].reshape(16, 128, 8).transpose(1, 0, 2).reshape(128, 128),
    ], axis=1)
    gate_b = np.ascontiguousarray(a["cd_gate_b"].reshape(2, 4).T)
    rg_w = np.stack([a["rg_wa"][0], a["rg_wx"][0]]).transpose(2, 0, 1, 3).reshape(128, 2048)

    n = np.arange(128)
    back = n[:, None] - n[None, :]
    causal = np.where(back >= 0, -back, -1e34).astype(np.float32)
    distance = np.concatenate([causal, -(back + 128).astype(np.float32), causal], axis=1)
    later = np.where(n[:, None] > n[None, :], 1e30, 0.0).astype(np.float32)
    future = np.concatenate([later, np.zeros((128, 128), np.float32), later], axis=1)
    select = np.zeros((128, 4, 128), np.float32)
    for h in range(4):
        select[h, h] = 1.0
    tables = np.concatenate([np.eye(128, dtype=np.float32), np.ones((128, 256), np.float32)], axis=1)
    futures = np.concatenate([future, select.reshape(128, 512)], axis=1)

    arrays = {"x_t": a["x"][0].T, "weights": weights, "mod_weights": mod_weights, "vectors": vectors,
              "tables": tables, "distances": distance, "futures": futures, "gate_b": gate_b, "rg_w": rg_w}
    arrays = {k: np.ascontiguousarray(w) for k, w in arrays.items()}
    nc = bacc.Bacc("TRN2", target_bir_lowering=False, num_devices=1, dynamic_dma_scratch_size=1024)
    args = [nc.dram_tensor(k, w.shape, F32, kind="ExternalInput").ap() for k, w in arrays.items()]
    out = nc.dram_tensor("out_t", (D, T), F32, kind="ExternalOutput").ap()
    trunk(nc, *args, out)
    r = run_bass_kernel_spmd(nc, [arrays], core_ids=[0])
    return np.ascontiguousarray(r.results[0]["out_t"].T)[None]
```

```python
from contextlib import ExitStack

import concourse.bass as bass
from concourse import mybir

F32 = mybir.dt.float32
F32R = mybir.dt.float32r
ALU = mybir.AluOpType
ACT = mybir.ActivationFunctionType
AX = mybir.AxisListType

P = 128
T = 256
D = 2048
KD = D // P
FFN = 5632
KF = FFN // P
HEADS_A = 8
HEADS_D = 4
TILES_D = 2
CHUNK_K = 2
GROUP = 4
RING = 4
MOD_GROUPS = 48
MOD_CHUNKS = KD // CHUNK_K
EPS = 1e-6

VECTORS = {}
_at = 0
for _name, _n in (("cond", KD), ("mod_b", 192), ("gain", 5 * KD), ("ab_conv", 24), ("rg_conv", 32),
                  ("rg_conv_b", 8), ("rg_ba", 8), ("rg_bx", 8), ("rg_lambda", 8), ("w_gates", KD * 8)):
    VECTORS[_name] = (_at, _at + _n)
    _at += _n
N_VECTORS = _at
TABLES = {}
_at = 0
for _name, _n in (("ident", P), ("ones", T), ("mean", P)):
    TABLES[_name] = (_at, _at + _n)
    _at += _n
N_TABLES = _at


class Gemm:

    def __init__(self, kind, ktiles, mods, loop=None, after=None, drained=False, fed=None):
        self.kind, self.bodies, self.mods, self.loop = kind, len(mods), mods, loop
        self.n = ktiles // CHUNK_K
        self.before = after if not drained else None
        self.fed = fed
        self.begins = after is None
        self.quad0 = after.quad0 + after.bodies * after.n // 2 if after else 0
        self.tile0 = after.tile0 + after.bodies * 2 * GROUP if after else 0
        self.group0 = after.group0 + sum(after.mods) if after else 8

    def parts(self):
        lo, hi = self.loop or (self.bodies, self.bodies)
        return [*range(lo), *([(lo, hi)] if self.loop else []), *range(hi, self.bodies)]

    def m(self, i):
        return self.mods[i] if isinstance(i, int) else self.mods[self.loop[0]]

    def offset(self, half):
        return (half * self.n) % RING

    def quads(self, i, half):
        return self.quad0 + i * (self.n // 2) + (half * self.n - self.offset(half)) // RING

    def tiles(self, i, half):
        return self.tile0 + i * (2 * GROUP) + half * GROUP

    def groups(self, i, half):
        m = self.m(i)
        inside = half * (m // 2)
        if isinstance(i, int):
            return self.group0 + sum(self.mods[:i]) + inside
        lo = self.loop[0]
        return self.group0 + sum(self.mods[:lo]) + (i - lo) * m + inside

    def mod_chunk(self, i, half, j):
        m = self.m(i)
        if m == 1 and self.begins and isinstance(i, int) and i == 0:
            return (0, j) if half else None
        if m == 1 and j % 2 == 1:
            return 0, half * 4 + j // 2
        if m == 2 and j < MOD_CHUNKS:
            return 0, j
        if m == 4 and j < 8:
            return 0, j
        if m == 4 and 12 <= j < 20:
            return 1, j - 12
        return None

    def reduced_after(self, i, half, j):
        m = self.m(i)
        if (m == 1 and half == 1 and j == 6) or (m == 2 and j == min(8, self.n - 2)) or (m == 4 and j == 8):
            return 0
        if m == 4 and j == 20:
            return 1
        return None

    def carries(self, i, half):
        return self.m(i) in (2, 4) or (self.m(i) == 1 and half == 1)

    def previous(self, i, half):
        if half:
            return (self, i, 0), self.carries(i, 0)
        if isinstance(i, int) and i == 0:
            if self.before is None:
                return None, False
            last = self.before.bodies - 1
            return (self.before, last, 1), self.before.carries(last, 1)
        before = i - 1 if isinstance(i, int) else self.loop[0] - 1
        return (self, i - 1, 1), self.carries(before, 1)


def plan():
    ab = Gemm("store", KD, [1, 1, 1, 2, 2, 2], loop=(1, 3), fed=0)
    ab_out = Gemm("residual", KD, [1, 2], after=ab, fed=1)
    up0 = Gemm("swiglu", KD, [1] * 11, loop=(2, 11), after=ab_out, drained=True, fed=2)
    down0 = Gemm("residual", KF, [4, 2], after=up0)
    cd = Gemm("store", KD, [1] * 6, after=down0, drained=True, fed=3)
    cd_out = Gemm("residual", KD, [1, 1], after=cd, fed=4)
    up1 = Gemm("swiglu", KD, [1, 1, 1] + [0] * 8, loop=(4, 11), after=cd_out, drained=True, fed=5)
    down1 = Gemm("residual", KF, [0, 0], after=up1)
    assert up1.group0 + sum(up1.mods) == MOD_GROUPS
    return ab, ab_out, up0, down0, cd, cd_out, up1, down1


def wait(eng, sem, value):
    if not isinstance(value, int) or value > 0:
        eng.wait_ge(sem, value)


def trunk(nc, x_t, weights, mod_weights, vectors, tables, distances, futures, gate_b, rg_w, out_t):
    ab, ab_out, up0, down0, cd, cd_out, up1, down1 = plan()
    gemms = (ab, ab_out, up0, down0, cd, cd_out, up1, down1)

    with ExitStack() as ctx:
        def sb(name, shape, dt=F32):
            return ctx.enter_context(nc.sbuf_tensor(name, shape, dt))

        def sem(name):
            return ctx.enter_context(nc.semaphore(name))

        raw = sb("raw", [P, RING, CHUNK_K, GROUP * P])
        high = sb("high", [P, RING, CHUNK_K, GROUP * P], F32R)
        low = sb("low", [P, RING, CHUNK_K, GROUP * P], F32R)
        mod_raw = sb("mod_raw", [P, RING, CHUNK_K, GROUP * P])
        mod_acc = sb("mod_acc", [P, CHUNK_K, GROUP * P])
        mod = sb("mod", [P, 4 * MOD_GROUPS])
        x = sb("x", [P, KD, T])
        acts = sb("acts", [P, KD, 2, T], F32R)
        cross = sb("cross", [P, GROUP, T])
        summed = sb("summed", [P, GROUP, T])
        gate = sb("gate", [P, GROUP, T])
        vec = sb("vec", [P, N_VECTORS])
        tab = sb("tab", [P, N_TABLES])
        cond = sb("cond", [P, KD])
        norm_gain = sb("norm_gain", [P, KD])
        gates_w = sb("gates_w", [P, KD, 2, 8], F32R)
        small = sb("small", [P, 97])
        gbias = sb("gbias", [4, 2])
        with nc.sbuf_tensor("mixer", [P, 2 * KF, T], F32) as mixer:
            pass
        hidden = sb("hidden", [P, KF, 2, T], F32R)

        bank = [ctx.enter_context(nc.psum_tensor(f"bank{b}", [P, 512], F32)) for b in range(8)]

        raw_landed = [sem(f"raw_landed{s}") for s in range(RING)]
        mod_landed = [sem(f"mod_landed{s}") for s in range(RING)]
        x_landed = sem("x_landed")
        vectors_landed = sem("vectors_landed")
        tables_landed = sem("tables_landed")
        rg_landed = sem("rg_landed")
        futures_landed = sem("futures_landed")
        out_landed = sem("out_landed")
        high_ready = sem("high_ready")
        low_ready = sem("low_ready")
        low_ready_pool = sem("low_ready_pool")
        chunk_used = sem("chunk_used")
        tile_multiplied = sem("tile_multiplied")
        cross_copied = sem("cross_copied")
        tile_out = sem("tile_out")
        x_updated = sem("x_updated")
        x_squared = sem("x_squared")
        squares_added = sem("squares_added")
        gate_ready = sem("gate_ready")
        hidden_ready = sem("hidden_ready")
        hidden_high = sem("hidden_high")
        hidden_low = sem("hidden_low")
        cond_ready = sem("cond_ready")
        mod_added = sem("mod_added")
        mod_folded = sem("mod_folded")
        rms_ready = sem("rms_ready")
        mod_reduced = sem("mod_reduced")
        mod_ready = sem("mod_ready")
        square_sum = sem("square_sum")
        normed_ready = sem("normed_ready")
        diagonal_ready = sem("diagonal_ready")
        inverse_ready = sem("inverse_ready")
        gain_ready = sem("gain_ready")
        feed_high = sem("feed_high")
        feed_low = sem("feed_low")
        normalised = sem("normalised")
        dve_step = sem("dve_step")
        act_step = sem("act_step")
        v_turned = sem("v_turned")
        v_stored = sem("v_stored")
        bias_ready = sem("bias_ready")
        scores_ready = sem("scores_ready")
        scores_max = sem("scores_max")
        probs_exp = sem("probs_exp")
        probs_ready = sem("probs_ready")
        probs_turned = sem("probs_turned")
        probs_stored = sem("probs_stored")
        heads_out = sem("heads_out")
        heads_stored = sem("heads_stored")
        conv_ready = sem("conv_ready")
        gates_high = sem("gates_high")
        gates_split = sem("gates_split")
        gates_done = sem("gates_done")
        gates_copied = sem("gates_copied")
        gates_summed = sem("gates_summed")
        gates_rows = sem("gates_rows")
        f_rows = sem("f_rows")
        f_exp = sem("f_exp")
        f_exp1 = sem("f_exp1")
        f_log = sem("f_log")
        m_rows = sem("m_rows")
        m_exp = sem("m_exp")
        a_turned = sem("a_turned")
        a_stored = sem("a_stored")
        lam_exp = sem("lam_exp")
        lam_exp1 = sem("lam_exp1")
        lam_log = sem("lam_log")
        rg_conv_ready = sem("rg_conv_ready")
        rg_products = sem("rg_products")
        rg_sigmoid = sem("rg_sigmoid")
        log_a_ready = sem("log_a_ready")
        a_ready = sem("a_ready")
        u_square = sem("u_square")
        u_root = sem("u_root")
        gelu_ready = sem("gelu_ready")
        rg_y_ready = sem("rg_y_ready")
        og_ready = sem("og_ready")
        m_spread = sem("m_spread")
        w_minus = sem("w_minus")
        w_exp = sem("w_exp")
        qk_ready = sem("qk_ready")
        p_ready = sem("p_ready")
        num_ready = sem("num_ready")
        den_abs = sem("den_abs")
        head_done = sem("head_done")
        mlstm_y_ready = sem("mlstm_y_ready")

        def v(name):
            a, b = VECTORS[name]
            return vec[:, a:b]

        def t(name):
            a, b = TABLES[name]
            return tab[:, a:b]

        ident, ones, mean = t("ident"), t("ones")[:, 0:P], t("mean")
        gate_flat = gate[:].rearrange("p a t -> p (a t)")
        distance, future = gate_flat[:, 0:384], gate_flat[:, 0:384]
        select = gate_flat[0:4, 384:896].rearrange("p (h m) -> p h m", h=HEADS_D)
        pick = gate_flat[0:16, 896:904]
        gate_cross, gate_sums = summed[0:16, 2], summed[0:16, 3]
        square, square_acc = gate[:, 0:2], gate[:, 2]
        gain = v("gain").rearrange("p (n j) -> p n j", j=KD)
        w_gates = v("w_gates").rearrange("p (k n) -> p k n", n=8)
        rms, inv_rms = mixer[:, 32], mixer[:, 33]
        rms_columns, inv_columns, diagonal = small[:, 88:90], small[:, 90:92], mixer[:, 32]
        x_view = x_t.rearrange("(j p) t -> p j t", p=P)
        out_view = out_t.rearrange("(j p) t -> p j t", p=P)

        def mod_part(layer, part):
            c = (layer * 6 + part) * KD
            return mod[:, c:c + KD]

        def shift_column(gm, k):
            n, layer, part = norms[gm]
            c = k // GROUP * 8 + GROUP + k % GROUP if n == 0 else (layer * 6 + part) * KD + k
            return mod[:, c:c + 1]

        def tiles(a, b):
            return mixer[:, a:b, :]

        def flat(a, b):
            return mixer[:, a:b, :].rearrange("p a t -> p (a t)")

        V_A = 16
        def probs(h):
            return flat(56 + 2 * (h % 2), 58 + 2 * (h % 2))[:, 0:384]

        def bias(h):
            return flat(60 + 2 * (h % 2), 62 + 2 * (h % 2))[:, 0:384]

        def probs_t(h):
            return flat(84 + 2 * (h % 2), 86 + 2 * (h % 2))[:, 0:384]

        v_rows = mixer[:, 48:56, :].rearrange("p (s a) t -> p s (a t)", s=2)
        taps = v("ab_conv").rearrange("p (g k) -> p g k", k=3)

        Q_D, K_D, V_D, G_RG, OG = 8, 16, 24, 32, 40
        rg_blocks = flat(56, 64).rearrange("p (n g j) -> p n g j", n=2, g=8)
        rtaps = v("rg_conv").rearrange("p (g k) -> p g k", k=4)

        def row(n):
            return summed[0:4, n, :]

        def decay(h):
            return flat(56 + 2 * (h % 2), 58 + 2 * (h % 2))[:, 0:384]

        def den(h):
            return mixer[:, 60 + h % 2, :]

        def weighted(h):
            return flat(K_D + 2 * h, K_D + 2 * h + 2)[:, 0:384]

        def y_pair(gm, j):
            at = (2 * j if j < 4 else 72 + 2 * (j - 4)) if gm is ab_out else (64 + 2 * j if j < 4 else Q_D + 2 * (j - 4))
            return tiles(at, at + 2)

        norms = {ab: (0, 0, 0), up0: (1, 0, 3), cd: (2, 1, 0), up1: (3, 1, 3)}
        final_norm = 4

        def chunk_low(gm, i, half, j):
            jj = j + gm.offset(half)
            q = gm.quads(i, half) + jj // RING
            return low_ready_pool if jj % 2 else low_ready, q * (RING // 2) + jj % RING // 2 + 1

        RESIDUALS = {ab_out: 0, down0: 1, cd_out: 2, down1: 3}

        def residual_tile(gm, i, half, f):
            return RESIDUALS[gm] * KD + i * 8 + half * GROUP + f

        def prefilled(gm):
            return gm in norms and gm is not ab

        def is_drained(gm, i, half):
            return gm in RESIDUALS and (i, half) == (gm.bodies - 1, 1)

        def fed_by(gm, i, half):
            if gm in (ab, cd) and isinstance(i, int) and (i, half) == (gm.bodies - 1, 1):
                return ab_out if gm is ab else cd_out
            return None

        def accumulator(acc, k):
            return acc[:, k] if acc is mod_acc else acc[:, k * 2:k * 2 + 2].rearrange("p a t -> p (a t)")

        square_bank, inverse_bank = bank[5], bank[6]

        def idle(half, n):
            return bank[4 * (1 - half) + n]

        def head_bank(h, n):
            half, first = ((1, 0), (0, 0), (0, 2), (1, 0))[h]
            return idle(half, first + n)

        block = ctx.enter_context(nc.Block())

        @block.sync
        def _(sp):
            def load_raw(gm, i, half, j):
                jj = j + gm.offset(half)
                g = gm.quads(i, half) * RING + jj
                s, count = chunk_low(gm, i, half, j)
                wait(sp, s, count - RING // 2)
                sp.dma_start(raw[:, jj % RING], weights[bass.ds(g, 1)].rearrange(
                    "g p (k n) -> p (g k) n", k=CHUNK_K)).then_inc(raw_landed[jj % RING], 16)

            def load_mod(group, j):
                g = group * MOD_CHUNKS + j
                wait(sp, mod_added, g - RING + 1)
                sp.dma_start(mod_raw[:, j % RING], mod_weights[bass.ds(g, 1)].rearrange(
                    "g p (k n) -> p (g k) n", k=CHUNK_K)).then_inc(mod_landed[j % RING], 16)

            sp.dma_start(vec[:], vectors).then_inc(vectors_landed, 16)
            for j in range(MOD_CHUNKS):
                load_mod(0, j)
            sp.dma_start(tab[:], tables).then_inc(tables_landed, 16)
            sp.dma_start(gate_flat[:, 0:384], distances).then_inc(tables_landed, 16)
            sp.dma_start(gbias[:], gate_b).then_inc(tables_landed, 16)
            sp.dma_start(x[:], x_view).then_inc(x_landed, 16)

            def first_half():
                for q in range(4):
                    if q:
                        for j in range(MOD_CHUNKS):
                            load_mod(2 * q, j)
                    for j in (2 * q, 2 * q + 1):
                        load_raw(ab, 0, 0, j)
                    for j in range(MOD_CHUNKS):
                        load_mod(2 * q + 1, j)

            def body(gm, i):
                for half in range(2):
                    if gm is ab and isinstance(i, int) and (i, half) == (0, 0):
                        first_half()
                        continue
                    for j in range(gm.n):
                        m = gm.mod_chunk(i, half, j)
                        if m:
                            load_mod(gm.groups(i, half) + m[0], m[1])
                        load_raw(gm, i, half, j)
                        if gm is cd and (i, half, j) == (0, 0, 3):
                            sp.wait_ge(tile_out, gm.tile0)
                            sp.wait_ge(square_sum, 3)
                            sp.dma_start(flat(56, 64), rg_w).then_inc(rg_landed, 16)
                            sp.dma_start(gate_flat[:, 0:904], futures).then_inc(futures_landed, 16)

            for gm in gemms:
                for part in gm.parts():
                    if isinstance(part, int):
                        body(gm, part)
                    else:
                        with sp.Fori(*part) as i:
                            body(gm, i)

            parts = ((0, 2), (2, 6), (6, 10), (10, 14), (14, 16))
            for a, b in parts:
                sp.wait_ge(normalised, b)
                sp.dma_start(out_view[:, a:b], tiles(a, b)).then_inc(out_landed, 16)
            sp.wait_ge(out_landed, 16 * len(parts))

        @block.gpsimd
        def _(pool):
            def split(gm, i, half, j, ready=low_ready_pool):
                jj = j + gm.offset(half)
                s = jj % RING
                pool.wait_ge(high_ready, gm.quads(i, half) * RING + jj + 1)
                nc.gpsimd.tensor_tensor(low[:, s], raw[:, s], high[:, s].bitcast(F32),
                                        ALU.subtract).then_inc(ready, 1)

            def fold(group, acc=mod_acc):
                pool.wait_ge(mod_added, (group + 1) * MOD_CHUNKS)
                a = accumulator(acc, 0)
                nc.gpsimd.tensor_tensor(a, a, accumulator(acc, 1), ALU.add).then_inc(mod_folded, 1)

            def first_half():
                for q in range(4):
                    fold(2 * q, cross)
                    split(ab, 0, 0, 2 * q, low_ready)
                    split(ab, 0, 0, 2 * q + 1)
                    fold(2 * q + 1, summed)
                    if q == 0:
                        pool.wait_ge(inverse_ready, 1)
                        for k in range(KD):
                            nc.gpsimd.tensor_tensor(mixer[:, k], x[:, k], inv_rms,
                                                    ALU.mult).then_inc(normed_ready, 1)

            def body(gm, i):
                for half in range(2):
                    if gm is ab and isinstance(i, int) and (i, half) == (0, 0):
                        first_half()
                        continue
                    for j in range(gm.n):
                        jj = j + gm.offset(half)
                        if jj % 2:
                            split(gm, i, half, j)
                        m = gm.mod_chunk(i, half, j)
                        if m and m[1] == MOD_CHUNKS - 1:
                            fold(gm.groups(i, half) + m[0])

            for gm in gemms:
                for part in gm.parts():
                    if isinstance(part, int):
                        body(gm, part)
                    else:
                        with pool.Fori(*part) as i:
                            body(gm, i)

        @block.scalar
        def _(act):
            steps = [0]

            def link(ins):
                steps[0] += 1
                ins.then_inc(act_step, 1)
                act.wait_ge(act_step, steps[0])

            def split_high(gm, i, half, j):
                jj = j + gm.offset(half)
                q = gm.quads(i, half)
                act.wait_ge(raw_landed[jj % RING], q * 16 + 16 * (jj // RING + 1))
                wait(act, chunk_used, q * RING + jj - RING + 1)
                nc.scalar.activation(high[:, jj % RING], raw[:, jj % RING], ACT.Copy).then_inc(high_ready, 1)

            def copy_cross(gm, i, half, f):
                wait(act, tile_out, gm.tiles(i, half) + f - GROUP + 1)
                nc.scalar.copy(cross[:, f], bank[4 * half + f][:, T:2 * T]).then_inc(cross_copied, 1)

            def after_tile(gm, i, half, f):
                if gm.kind == "swiglu" and half == 0:
                    act.wait_ge(tile_out, gm.tiles(i, 0) + f + 1)
                    nc.scalar.activation(gate[:, f], gate[:, f], ACT.Silu).then_inc(gate_ready, 1)
                elif gm.kind == "swiglu":
                    h0 = 0 if gm is up0 else KF
                    act.wait_ge(hidden_ready, h0 + i * GROUP + f + 1)
                    nc.scalar.activation(hidden[:, bass.ds(i * GROUP + f, 1), 0], summed[:, f:f + 1],
                                         ACT.Copy).then_inc(hidden_high, 1)
                elif gm.kind == "residual":
                    n = residual_tile(gm, i, half, f)
                    act.wait_ge(x_updated, n + 1)
                    if n % KD < 2:
                        act.wait_ge(square_sum, n // KD + 1)
                    else:
                        act.wait_ge(squares_added, n // KD * (KD - 1) + n % KD - 1)
                    nc.scalar.activation(square[:, n % 2], x[:, n % KD], ACT.Square).then_inc(x_squared, 1)

            def first_half():
                for q in range(4):
                    for j in (2 * q, 2 * q + 1):
                        split_high(ab, 0, 0, j)
                    for j in (2 * q, 2 * q + 1):
                        feed(ab, j)

            def body(gm, i):
                for half in range(2):
                    before, _ = gm.previous(i, half)
                    first = isinstance(i, int) and (i, half) == (0, 0)
                    if first and gm is ab:
                        first_half()
                        continue
                    for j in range(gm.n):
                        if first and gm.fed is not None and j >= RING:
                            feed(gm, j)
                        if not (first and j < RING and prefilled(gm)):
                            split_high(gm, i, half, j)
                        if fed_by(gm, i, half) and j >= RING:
                            feed(fed_by(gm, i, half), j - RING)
                        if before and 2 <= j < 2 + GROUP:
                            if j == 2:
                                act.wait_ge(chunk_used, gm.quads(i, half) * RING + gm.offset(half))
                            copy_cross(*before, j - 2)
                        if before and 3 <= j < 3 + GROUP:
                            after_tile(*before, j - 3)
                        if gm in (ab, cd) and isinstance(i, int):
                            mixer_step(gm, 2 * i + half, half, j)
                        if gm is cd_out and first and j == 5:
                            act.wait_ge(tile_out, cd_out.tile0)
                            nc.scalar.activation(tiles(OG + 4, OG + 8), tiles(OG + 4, OG + 8),
                                                 ACT.Sigmoid).then_inc(og_ready, 1)

            def gemm(gm):
                if prefilled(gm):
                    root(norms[gm][0])
                    split_high(gm, 0, 0, 2)
                    feed(gm, 0)
                    feed(gm, 1)
                    split_high(gm, 0, 0, 3)
                    feed(gm, 2)
                    feed(gm, 3)
                for part in gm.parts():
                    if isinstance(part, int):
                        body(gm, part)
                    else:
                        with act.Fori(*part) as i:
                            body(gm, i)

            def drain(gm, following=None):
                last = gm.bodies - 1
                nc.scalar.activation(small[:, 96:97], small[:, 95:96], ACT.Sqrt)
                if following:
                    for j in range(2):
                        split_high(following, 0, 0, j)
                for f in range(GROUP):
                    if f < GROUP - 1:
                        act.wait_ge(tile_multiplied, RESIDUALS[gm] * (GROUP - 1) + f + 1)
                    else:
                        act.wait_ge(chunk_used, (gm.quad0 + gm.bodies * gm.n // 2) * RING)
                    copy_cross(gm, last, 1, f)
                    if f:
                        after_tile(gm, last, 1, f - 1)
                after_tile(gm, last, 1, GROUP - 1)

            def root(n):
                act.wait_ge(square_sum, n + 1)
                to, columns = (rms_columns, 2) if n else (rms, T)
                nc.scalar.activation(to, square_bank[:, 0:columns], ACT.Sqrt,
                                     bias=small[:, 95:96]).then_inc(rms_ready, 1)

            def feed(gm, j):
                if gm in norms:
                    for k in (2 * j, 2 * j + 1):
                        act.wait_ge(normed_ready, norms[gm][0] * KD + k + 1)
                        if gm is ab:
                            act.wait_ge(gain_ready, k // GROUP + 1)
                            nc.scalar.activation(acts[:, k, 0], mixer[:, k], ACT.Identity,
                                                 bias=shift_column(gm, k),
                                                 scale=norm_gain[:, k:k + 1]).then_inc(feed_high, 1)
                            continue
                        nc.scalar.activation(acts[:, k, 0], mixer[:, k], ACT.Identity,
                                             bias=shift_column(gm, k)).then_inc(feed_high, 1)
                else:
                    if j >= 4:
                        act.wait_ge(*((conv_ready, 1 if j < 6 else 2) if gm is ab_out
                                      else (mlstm_y_ready, 1 if j < 6 else 2)))
                    else:
                        act.wait_ge(*((heads_stored, 2 * j + 2) if gm is ab_out else (rg_y_ready, 1)))
                    nc.scalar.activation(acts[:, 2 * j:2 * j + 2, 0], y_pair(gm, j), ACT.Copy).then_inc(feed_high, 2)

            def copy_values(b, half, n):
                act.wait_ge(v_turned, b + 1)
                q = b % 4
                nc.scalar.copy(v_rows[:, q // 2, 512 * (q % 2):512 * (q % 2) + 512],
                               idle(half, n)[:]).then_inc(v_stored, 1)

            def mixer_step(gm, n, half, j):
                if gm is ab:
                    attention_step(n, half, j)
                else:
                    layer1_step(n, half, j)

            def attention_step(n, half, j):
                if n == 6 and j == 7:
                    for b in range(2):
                        copy_values(b, half, b)
                if n == 7 and j == 1:
                    for b in range(2):
                        copy_values(2 + b, 1 - half, b)
                if 7 <= n <= 10 and j == 7:
                    for h in (2 * (n - 7), 2 * (n - 7) + 1):
                        act.wait_ge(probs_turned, h + 1)
                        wait(act, heads_out, h - 1)
                        nc.scalar.copy(probs_t(h), idle(half, h % 2)[:, 0:384]).then_inc(probs_stored, 1)
                if 6 <= n <= 9 and j == 6:
                    act.wait_ge(tables_landed, 48)
                    for h in (2 * (n - 6), 2 * (n - 6) + 1):
                        wait(act, scores_max, h - 1)
                        nc.scalar.mul(bias(h), distance, 2.0 ** (-8.0 * (h + 1) / HEADS_A)).then_inc(bias_ready, 1)
                if 6 <= n <= 9 and j == 7:
                    for h in (2 * (n - 6), 2 * (n - 6) + 1):
                        act.wait_ge(scores_max, h + 1)
                        for q, (a, b) in enumerate(((0, 128), (128, 384))):
                            c = 2 * h + q
                            nc.scalar.activation(probs(h)[:, a:b], probs(h)[:, a:b], ACT.Exp, bias=small[:, c:c + 1],
                                                 accum_out=small[:, 16 + c:17 + c]).then_inc(probs_exp, 1)
                if 8 <= n <= 11 and j == 1:
                    for h in (2 * (n - 8), 2 * (n - 8) + 1):
                        act.wait_ge(heads_out, h + 1)
                        nc.scalar.copy(mixer[:, h], idle(1 - half, h % 2)[:, 0:T]).then_inc(heads_stored, 1)

            def rg_gates(gs, half):
                for g, b in gs:
                    act.wait_ge(rg_products, g + 1)
                    for q, (name, at) in enumerate((("rg_ba", 72), ("rg_bx", 80))):
                        nc.scalar.activation(mixer[:, at + g], idle(half, b)[:, q * T:q * T + T], ACT.Sigmoid,
                                             bias=v(name)[:, g:g + 1]).then_inc(rg_sigmoid, 1)

            def layer1_step(n, half, j):
                if (n, j) == (0, 6):
                    nc.scalar.activation(gates_w[:, :, 0], w_gates, ACT.Copy).then_inc(gates_high, 1)
                if (n, j) == (1, 7):
                    act.wait_ge(gates_done, 1)
                    nc.scalar.copy(gate_cross, idle(half, 0)[0:16, T:2 * T]).then_inc(gates_copied, 1)
                if (n, j) == (2, 1):
                    link(nc.scalar.activation(small[:, 40:48], v("rg_lambda"), ACT.Abs))
                    nc.scalar.activation(small[:, 40:48], small[:, 40:48], ACT.Exp, scale=-1.0).then_inc(lam_exp, 1)
                if (n, j) == (2, 3):
                    act.wait_ge(lam_exp1, 1)
                    nc.scalar.activation(small[:, 48:56], small[:, 40:48], ACT.Ln).then_inc(lam_log, 1)
                if (n, j) == (3, 0):
                    act.wait_ge(f_rows, 1)
                    link(nc.scalar.activation(row(2), row(1), ACT.Abs))
                    nc.scalar.activation(row(2), row(2), ACT.Exp, scale=-1.0).then_inc(f_exp, 1)
                if (n, j) == (3, 2):
                    act.wait_ge(f_exp1, 1)
                    nc.scalar.activation(row(2), row(2), ACT.Ln).then_inc(f_log, 1)
                if (n, j) == (3, 6):
                    act.wait_ge(m_rows, 1)
                    nc.scalar.activation(row(3), row(2), ACT.Exp, scale=-1.0).then_inc(m_exp, 1)
                if (n, j) == (4, 7):
                    rg_gates(((0, 0), (1, 1), (2, 2)), half)
                if (n, j) == (5, 7):
                    rg_gates(((3, 0), (4, 1), (5, 2)), half)
                if (n, j) == (6, 0):
                    rg_gates(((6, 0), (7, 1)), 1 - half)
                if n in (6, 7) and j == 7:
                    for h in (2 * (n - 6), 2 * (n - 6) + 1):
                        act.wait_ge(w_minus, h + 1)
                        nc.scalar.activation(decay(h), decay(h), ACT.Exp, scale=-1.0).then_inc(w_exp, 1)
                if (n, j) == (7, 1):
                    act.wait_ge(log_a_ready, 1)
                    link(nc.scalar.activation(tiles(0, 8), tiles(72, 80), ACT.Exp))
                    nc.scalar.activation(tiles(72, 80), tiles(72, 80), ACT.Tanh, scale=-1.0).then_inc(a_ready, 1)
                if (n, j) == (8, 0):
                    act.wait_ge(u_square, 1)
                    nc.scalar.activation(tiles(64, 72), tiles(64, 72), ACT.Sqrt).then_inc(u_root, 1)
                if (n, j) == (8, 7):
                    for b in range(2):
                        copy_values(4 + b, half, b)
                if (n, j) == (9, 1):
                    for b in range(2, 4):
                        copy_values(4 + b, 1 - half, b)
                for h in {9: (0,), 10: (1, 2), 11: (3,)}.get(n, ()) if j == 7 else ():
                    act.wait_ge(num_ready, h + 1)
                    wait(act, head_done, h - 1)
                    nc.scalar.activation(den(h), head_bank(h, 0)[:, 0:T], ACT.Abs).then_inc(den_abs, 1)
                if (n, j) == (10, 6):
                    act.wait_ge(tile_out, cd.tiles(5, 0))
                    nc.scalar.activation(tiles(G_RG, G_RG + 8), tiles(G_RG, G_RG + 8),
                                         ACT.Gelu_apprx_tanh).then_inc(gelu_ready, 1)
                if (n, j) == (11, 6):
                    act.wait_ge(tile_out, cd.tiles(5, 1))
                    nc.scalar.activation(tiles(OG, OG + 4), tiles(OG, OG + 4), ACT.Sigmoid).then_inc(og_ready, 1)

            act.wait_ge(vectors_landed, 16)
            nc.scalar.activation(cond[:], v("cond"), ACT.Silu).then_inc(cond_ready, 1)
            act.wait_ge(x_landed, 16)
            for j in range(4):
                nc.scalar.activation(tiles(16 + 4 * j, 20 + 4 * j), x[:, 4 * j:4 * j + 4],
                                     ACT.Square).then_inc(x_squared, 1)
            act.wait_ge(dve_step, 1)
            root(0)

            gemm(ab)
            gemm(ab_out)
            drain(ab_out, up0)
            gemm(up0)
            gemm(down0)
            drain(down0, cd)
            gemm(cd)
            gemm(cd_out)
            drain(cd_out, up1)
            gemm(up1)
            gemm(down1)
            drain(down1)
            root(final_norm)

        @block.vector
        def _(dve):
            steps = [0]

            def link(ins):
                steps[0] += 1
                ins.then_inc(dve_step, 1)
                dve.wait_ge(dve_step, steps[0])

            def split_low(gm, i, half, j):
                jj = j + gm.offset(half)
                s = jj % RING
                if s % 2:
                    return
                dve.wait_ge(high_ready, gm.quads(i, half) * RING + jj + 1)
                nc.vector.tensor_tensor(low[:, s], raw[:, s], high[:, s].bitcast(F32),
                                        ALU.subtract).then_inc(low_ready, 1)

            def add_mod(group, j, acc=mod_acc):
                s = j % RING
                dve.wait_ge(mod_landed[s], group * 32 + 16 * (j // RING + 1))
                for k in range(CHUNK_K):
                    w, cs = mod_raw[:, s, k], cond[:, 2 * j + k:2 * j + k + 1]
                    a = accumulator(acc, k)
                    if j == 0:
                        ins = nc.vector.tensor_scalar(a, w, cs, None, ALU.mult)
                    else:
                        if k == 0:
                            dve.wait_ge(mod_added, group * MOD_CHUNKS + j)
                        ins = nc.vector.scalar_tensor_tensor(a, w, cs, a, ALU.mult, ALU.add)
                ins.then_inc(mod_added, 1)

            def store_mod(group, b):
                dve.wait_ge(mod_reduced, group + 1)
                nc.vector.tensor_tensor(mod[:, bass.ds(group * 4, 4)], b[:, 0:4],
                                        v("mod_b")[:, bass.ds(group * 4, 4)], ALU.add).then_inc(mod_ready, 1)

            def first_half():
                for q in range(5):
                    for j in range(2 * MOD_CHUNKS):
                        if q < 4:
                            group = 2 * q + j // MOD_CHUNKS
                            if j % MOD_CHUNKS == 0:
                                wait(dve, mod_reduced, group - 1)
                            add_mod(group, j % MOD_CHUNKS, (cross, summed)[group % 2])
                        if (q, j) == (0, 12):
                            inverse(0)
                        if q == 0:
                            continue
                        if j == 2:
                            for group in (2 * q - 2, 2 * q - 1):
                                store_mod(group, bank[6 + group % 2])
                            dve.wait_ge(mod_ready, 2 * q)
                            scale, at = mod[:, 8 * q - 8:8 * q - 4], slice(4 * q - 4, 4 * q)
                            nc.vector.scalar_tensor_tensor(norm_gain[:, at], scale, 1.0, gain[:, 0, at],
                                                           ALU.add, ALU.mult).then_inc(gain_ready, 1)
                            dve.wait_ge(gain_ready, q)
                            dve.wait_ge(normed_ready, 4 * q)
                            for k in range(4 * q - 4, 4 * q):
                                ins = nc.vector.tensor_scalar(mixer[:, 48 + k], mixer[:, k], norm_gain[:, k:k + 1],
                                                              shift_column(ab, k), ALU.mult, ALU.add)
                            link(ins)
                        if j in (3, 4):
                            for k in range(4 * q - 4 + 2 * (j - 3), 4 * q - 2 + 2 * (j - 3)):
                                dve.wait_ge(feed_high, k + 1)
                                nc.vector.tensor_tensor(acts[:, k, 1], mixer[:, 48 + k], acts[:, k, 0].bitcast(F32),
                                                        ALU.subtract).then_inc(feed_low, 1)
                dve.wait_ge(low_ready, MOD_CHUNKS // 2)

            def tile_done(gm, i, half, f):
                tile = gm.tiles(i, half) + f
                dve.wait_ge(cross_copied, tile + 1)
                main = bank[4 * half + f][:, 0:T]
                if gm.kind == "store":
                    nc.vector.tensor_tensor(mixer[:, bass.ds(i * 8 + 4 * half + f, 1)],
                                            cross[:, f:f + 1], main.rearrange("p (a t) -> p a t", a=1),
                                            ALU.add).then_inc(tile_out, 1)
                elif gm.kind == "residual":
                    layer = 0 if gm in (ab_out, down0) else 1
                    gates = mod_part(layer, 2 if gm in (ab_out, cd_out) else 5)
                    nc.vector.tensor_tensor(summed[:, f], cross[:, f], main, ALU.add).then_inc(tile_out, 1)
                    dve.wait_ge(tile_out, tile + 1)
                    n = i * 8 + 4 * half + f
                    nc.vector.scalar_tensor_tensor(x[:, n], summed[:, f], gates[:, n:n + 1], x[:, n],
                                                   ALU.mult, ALU.add).then_inc(x_updated, 1)
                elif half == 0:
                    nc.vector.tensor_tensor(gate[:, f], cross[:, f], main, ALU.add).then_inc(tile_out, 1)
                else:
                    h0 = 0 if gm is up0 else KF
                    wait(dve, hidden_high, h0 + (i - 1) * GROUP + f + 1)
                    nc.vector.tensor_tensor(summed[:, f], cross[:, f], main, ALU.add).then_inc(tile_out, 1)
                    dve.wait_ge(tile_out, tile + 1)
                    dve.wait_ge(gate_ready, h0 + i * GROUP + f + 1)
                    nc.vector.tensor_tensor(summed[:, f], summed[:, f], gate[:, f],
                                            ALU.mult).then_inc(hidden_ready, 1)

            def after_tile(gm, i, half, f):
                if gm.kind == "swiglu" and half == 1:
                    h0 = 0 if gm is up0 else KF
                    dve.wait_ge(hidden_high, h0 + i * GROUP + f + 1)
                    n = i * GROUP + f
                    nc.vector.tensor_tensor(hidden[:, bass.ds(n, 1), 1], summed[:, f:f + 1],
                                            hidden[:, bass.ds(n, 1), 0].bitcast(F32),
                                            ALU.subtract).then_inc(hidden_low, 1)
                if gm.kind == "residual":
                    n = residual_tile(gm, i, half, f)
                    if n % KD == KD - 1:
                        return
                    dve.wait_ge(x_squared, 4 + n + 1)
                    if n % KD == 0:
                        ins = nc.vector.tensor_copy(square_acc, square[:, n % 2])
                    else:
                        dve.wait_ge(squares_added, n // KD * (KD - 1) + n % KD)
                        ins = nc.vector.tensor_tensor(square_acc, square_acc, square[:, n % 2], ALU.add)
                    ins.then_inc(squares_added, 1)

            def body(gm, i):
                for half in range(2):
                    groups = gm.groups(i, half)
                    before, carried = gm.previous(i, half)
                    first = isinstance(i, int) and (i, half) == (0, 0)
                    if first and gm is ab:
                        first_half()
                        continue
                    fetch = 0 if (gm is ab and isinstance(i, int) and i >= 3) or (gm is ab_out and first) else 2
                    for j in range(gm.n):
                        if first and gm.fed is not None and j >= RING:
                            feed(gm, j)
                        if not (first and j < RING and prefilled(gm)):
                            split_low(gm, i, half, j)
                        if fed_by(gm, i, half) and j >= RING:
                            feed(fed_by(gm, i, half), j - RING)
                        if j == fetch and carried:
                            store_mod(groups - 1, idle(1 - half, 3))
                        if j == 12 and gm.m(i) == 4:
                            store_mod(groups, idle(half, 3))
                        if before and 2 <= j < 2 + GROUP:
                            tile_done(*before, j - 2)
                        if before and 4 <= j < 4 + GROUP:
                            after_tile(*before, j - 4)
                        m = gm.mod_chunk(i, half, j)
                        if m:
                            if m[1] == 0:
                                dve.wait_ge(mod_reduced, groups + m[0])
                            add_mod(groups + m[0], m[1])
                        if gm in (ab, cd) and isinstance(i, int):
                            mixer_step(gm, 2 * i + half, half, j)
                        if first and gm is ab_out and j in (3, 4):
                            conv_tile(3 + j)
                        if first and gm is ab_out and j == 5:
                            dve.wait_ge(tile_out, ab_out.tile0)
                            link(nc.vector.tensor_tensor(tiles(76, 80), tiles(76, 80), tiles(44, 48), ALU.mult))
                            nc.vector.tensor_copy(small[:, 94:95], small[:, 95:96]).then_inc(conv_ready, 1)
                        if first and gm is cd_out and j == 5:
                            gate_heads(1)

            def gemm(gm):
                if prefilled(gm):
                    inverse(norms[gm][0])
                    for k in range(2):
                        normed(k)
                    feed(gm, 0)
                    feed(gm, 1)
                    split_low(gm, 0, 0, 2)
                    feed(gm, 2)
                    feed(gm, 3)
                for part in gm.parts():
                    if isinstance(part, int):
                        body(gm, part)
                    else:
                        with dve.Fori(*part) as i:
                            body(gm, i)

            def drain(gm, following=None):
                last = gm.bodies - 1
                if following:
                    split_low(following, 0, 0, 0)
                for f in range(GROUP):
                    tile_done(gm, last, 1, f)
                    if f:
                        after_tile(gm, last, 1, f - 1)
                after_tile(gm, last, 1, GROUP - 1)
                if gm.carries(last, 1):
                    store_mod(gm.groups(last, 1) + max(1, gm.m(last) // 2) - 1, bank[3])
                if following:
                    n, layer, part = norms[following]
                    dve.wait_ge(mod_ready, (layer * 6 + part + 2) * 4)
                    link(nc.vector.scalar_tensor_tensor(norm_gain[:], mod_part(layer, part + 1), 1.0,
                                                        gain[:, n], ALU.add, ALU.mult))

            def inverse(n):
                dve.wait_ge(rms_ready, n + 1)
                if n == 0:
                    nc.vector.reciprocal(inv_rms, rms).then_inc(inverse_ready, 1)
                    return
                link(nc.vector.reciprocal(inv_columns, rms_columns))
                for s in range(2):
                    ins = nc.vector.tensor_scalar(diagonal[:, s * P:s * P + P], ident, inv_columns[:, s:s + 1],
                                                  None, ALU.mult)
                ins.then_inc(diagonal_ready, 1)
                dve.wait_ge(inverse_ready, n + 1)

            def normed(k):
                nc.vector.scalar_tensor_tensor(mixer[:, k], x[:, k], norm_gain[:, k:k + 1], inverse_bank[:, 0:T],
                                               ALU.mult, ALU.mult).then_inc(normed_ready, 1)

            def low_part(gm, k):
                dve.wait_ge(feed_high, KD * gm.fed + k + 1)
                nc.vector.scalar_tensor_tensor(acts[:, k, 1], mixer[:, k], shift_column(gm, k),
                                               acts[:, k, 0].bitcast(F32), ALU.add,
                                               ALU.subtract).then_inc(feed_low, 1)

            def feed(gm, j):
                if gm in norms:
                    for k in (2 * j, 2 * j + 1):
                        if k + 2 < KD:
                            normed(k + 2)
                        low_part(gm, k)
                else:
                    dve.wait_ge(feed_high, KD * gm.fed + 2 * j + 2)
                    nc.vector.tensor_tensor(acts[:, 2 * j:2 * j + 2, 1], y_pair(gm, j),
                                            acts[:, 2 * j:2 * j + 2, 0].bitcast(F32),
                                            ALU.subtract).then_inc(feed_low, 2)

            def mixer_step(gm, n, half, j):
                if gm is ab:
                    attention_step(n, half, j)
                    conv_step(n, j)
                else:
                    layer1_step(n, half, j)

            def attention_step(n, half, j):
                if 6 <= n <= 9 and j == 7:
                    pair = (2 * (n - 6), 2 * (n - 6) + 1)
                    for h in pair:
                        p = probs(h)
                        dve.wait_ge(scores_ready, h + 1)
                        dve.wait_ge(bias_ready, h + 1)
                        wait(dve, probs_turned, h - 1)
                        link(nc.vector.scalar_tensor_tensor(p, idle(half, 2 + h % 2)[:, 0:384], float(P) ** -0.5,
                                                            bias(h), ALU.mult, ALU.add))
                        link(nc.vector.reduce_max(small[:, 2 * h:2 * h + 1], p[:, 0:128], AX.X, negate=True))
                        nc.vector.reduce_max(small[:, 2 * h + 1:2 * h + 2], p[:, 128:384], AX.X,
                                             negate=True).then_inc(scores_max, 1)
                    for h in pair:
                        p = probs(h)
                        dve.wait_ge(probs_exp, 2 * h + 2)
                        link(nc.vector.reciprocal(small[:, 32 + 2 * h:34 + 2 * h], small[:, 16 + 2 * h:18 + 2 * h]))
                        link(nc.vector.tensor_scalar(p[:, 0:128], p[:, 0:128], small[:, 32 + 2 * h:33 + 2 * h],
                                                     None, ALU.mult))
                        nc.vector.tensor_scalar(p[:, 128:384], p[:, 128:384], small[:, 33 + 2 * h:34 + 2 * h],
                                                None, ALU.mult).then_inc(probs_ready, 1)

            def conv_tile(g):
                u, y = mixer[:, 64 + g], mixer[:, 72 + g]
                link(nc.vector.tensor_scalar(y, u, taps[:, g, 2:3], None, ALU.mult))
                link(nc.vector.scalar_tensor_tensor(y[:, 1:T], u[:, 0:T - 1], taps[:, g, 1:2], y[:, 1:T],
                                                    ALU.mult, ALU.add))
                link(nc.vector.scalar_tensor_tensor(y[:, 2:T], u[:, 0:T - 2], taps[:, g, 0:1], y[:, 2:T],
                                                    ALU.mult, ALU.add))

            def conv_step(n, j):
                if (n, j) == (8, 6):
                    dve.wait_ge(tile_out, ab.tiles(4, 0))
                    link(nc.vector.tensor_tensor(tiles(64, 68), tiles(24, 28), tiles(28, 32), ALU.mult))
                if n == 10 and j in (5, 6):
                    conv_tile(2 * (j - 5))
                    conv_tile(2 * (j - 5) + 1)
                if (n, j) == (10, 7):
                    dve.wait_ge(tile_out, ab.tiles(4, 1))
                    nc.vector.tensor_tensor(tiles(72, 76), tiles(72, 76), tiles(32, 36), ALU.mult).then_inc(conv_ready, 1)
                if (n, j) == (11, 6):
                    dve.wait_ge(tile_out, ab.tiles(5, 1))
                    link(nc.vector.tensor_tensor(tiles(68, 72), tiles(36, 40), tiles(40, 44), ALU.mult))
                if (n, j) == (11, 7):
                    conv_tile(4)
                    conv_tile(5)

            def rg_conv_tile(g):
                u, y = mixer[:, g], mixer[:, 64 + g]
                link(nc.vector.tensor_scalar(y, u, rtaps[:, g, 3:4], v("rg_conv_b")[:, g:g + 1], ALU.mult, ALU.add))
                for k in range(2, -1, -1):
                    s = 3 - k
                    ins = nc.vector.scalar_tensor_tensor(y[:, s:T], u[:, 0:T - s], rtaps[:, g, k:k + 1], y[:, s:T],
                                                         ALU.mult, ALU.add)
                    if k:
                        link(ins)
                    else:
                        ins.then_inc(rg_conv_ready, 1)

            def gate_heads(q):
                dve.wait_ge(og_ready, q + 1)
                dve.wait_ge(head_done, 2 * q + 2)
                y = tiles(Q_D + 4 * q, Q_D + 4 * q + 4)
                nc.vector.tensor_tensor(y, y, tiles(OG + 4 * q, OG + 4 * q + 4), ALU.mult).then_inc(mlstm_y_ready, 1)

            def layer1_step(n, half, j):
                if (n, j) == (0, 7):
                    dve.wait_ge(gates_high, 1)
                    nc.vector.tensor_tensor(gates_w[:, :, 1], w_gates, gates_w[:, :, 0].bitcast(F32),
                                            ALU.subtract).then_inc(gates_split, 1)
                if (n, j) == (1, 7):
                    dve.wait_ge(gates_copied, 1)
                    nc.vector.tensor_tensor(gate_sums, gate_cross, idle(half, 0)[0:16, 0:T],
                                            ALU.add).then_inc(gates_summed, 1)
                if (n, j) == (2, 2):
                    dve.wait_ge(lam_exp, 1)
                    nc.vector.tensor_scalar(small[:, 40:48], small[:, 40:48], 1.0, None, ALU.add).then_inc(lam_exp1, 1)
                if (n, j) == (2, 4):
                    link(nc.vector.tensor_scalar(small[:, 32:40], v("rg_lambda"), -1.0, 0.0, ALU.mult, ALU.max))
                    dve.wait_ge(lam_log, 1)
                    link(nc.vector.tensor_tensor(small[:, 32:40], small[:, 32:40], small[:, 48:56], ALU.add))
                    link(nc.vector.tensor_scalar(small[:, 32:40], small[:, 32:40], -8.0, None, ALU.mult))
                if (n, j) == (2, 7):
                    dve.wait_ge(gates_rows, 1)
                    link(nc.vector.tensor_scalar(row(0), idle(half, 0)[0:4, 0:T], gbias[0:4, 0:1], None, ALU.add))
                    nc.vector.tensor_scalar(row(1), idle(half, 0)[0:4, T:2 * T], gbias[0:4, 1:2], None,
                                            ALU.add).then_inc(f_rows, 1)
                if (n, j) == (3, 1):
                    dve.wait_ge(f_exp, 1)
                    nc.vector.tensor_scalar(row(2), row(2), 1.0, None, ALU.add).then_inc(f_exp1, 1)
                if (n, j) == (3, 3):
                    dve.wait_ge(f_log, 1)
                    link(nc.vector.scalar_tensor_tensor(row(1), row(1), 0.0, row(2), ALU.min, ALU.subtract))
                    link(nc.vector.tensor_tensor_scan(row(3), t("ones")[0:4], row(1), 0.0, ALU.mult, ALU.add))
                    link(nc.vector.tensor_tensor(row(0), row(0), row(3), ALU.subtract))
                    link(nc.vector.tensor_tensor_scan(row(1), row(0), row(0), 0.0, ALU.max, ALU.max))
                    nc.vector.tensor_tensor(row(2), row(3), row(1), ALU.add).then_inc(m_rows, 1)
                if n == 2 and j >= 6:
                    dve.wait_ge(tile_out, cd.tiles(1, 0))
                    rg_conv_tile(j - 6)
                if n == 3 and j % 2 == 0:
                    rg_conv_tile(2 + j // 2)
                if n == 4 and j < 2:
                    rg_conv_tile(6 + j)
                if (n, j) == (5, 1):
                    dve.wait_ge(a_turned, 1)
                    nc.vector.tensor_copy(small[:, 80:88], idle(1 - half, 3)[:, 0:8]).then_inc(a_stored, 1)
                if (n, j) == (6, 4):
                    dve.wait_ge(rg_sigmoid, 16)
                    for g in range(8):
                        ins = nc.vector.tensor_scalar(mixer[:, 72 + g], mixer[:, 72 + g], small[:, 32 + g:33 + g],
                                                      None, ALU.mult)
                    ins.then_inc(log_a_ready, 1)
                    link(nc.vector.tensor_tensor(tiles(80, 88), tiles(80, 88), tiles(64, 72), ALU.mult))
                if n in (6, 7) and j == 7:
                    pair = (2 * (n - 6), 2 * (n - 6) + 1)
                    dve.wait_ge(futures_landed, 16)
                    dve.wait_ge(a_stored, 1)
                    spread = idle(half, 0)
                    for q, h in enumerate(pair):
                        dve.wait_ge(m_spread, h // 2 + 1)
                        wait(dve, p_ready, h - 1)
                        for s, (a, b) in enumerate(((0, 256), (256, 384))):
                            ins = nc.vector.scalar_tensor_tensor(
                                decay(h)[:, a:b], spread[:, q * T + s * P:q * T + T],
                                small[:, 80 + 4 * s + h:81 + 4 * s + h], future[:, a:b], ALU.subtract, ALU.add)
                        ins.then_inc(w_minus, 1)
                    for q, h in enumerate(pair):
                        dve.wait_ge(w_exp, h + 1)
                        dve.wait_ge(qk_ready, h + 1)
                        nc.vector.scalar_tensor_tensor(weighted(h), idle(half, 1 + q)[:, 0:384], 1.0 / 16.0, decay(h),
                                                       ALU.mult, ALU.mult).then_inc(p_ready, 1)
                if (n, j) == (7, 3):
                    dve.wait_ge(a_ready, 1)
                    link(nc.vector.tensor_tensor(tiles(64, 72), tiles(0, 8), tiles(0, 8), ALU.mult))
                    nc.vector.scalar_tensor_tensor(flat(64, 72), flat(64, 72), 1.0, flat(72, 80), ALU.add,
                                                   ALU.mult).then_inc(u_square, 1)
                if (n, j) == (8, 1):
                    dve.wait_ge(u_root, 1)
                    link(nc.vector.tensor_tensor(tiles(64, 72), tiles(64, 72), tiles(80, 88), ALU.mult))
                if n == 8 and 2 <= j < 6:
                    for g in (2 * (j - 2), 2 * (j - 2) + 1):
                        link(nc.vector.tensor_tensor_scan(mixer[:, 72 + g], mixer[:, g], mixer[:, 64 + g], 0.0,
                                                          ALU.mult, ALU.add))
                for h in {9: (0,), 10: (1, 2), 11: (3,)}.get(n, ()) if j == 7 else ():
                    dve.wait_ge(den_abs, h + 1)
                    link(nc.vector.tensor_tensor(den(h), den(h), head_bank(h, 0)[:, T:2 * T], ALU.max))
                    link(nc.vector.reciprocal(den(h), den(h)))
                    for e in range(TILES_D):
                        ins = nc.vector.tensor_tensor(mixer[:, Q_D + 2 * h + e],
                                                      head_bank(h, 1)[:, e * T:e * T + T], den(h), ALU.mult)
                    ins.then_inc(head_done, 1)
                if (n, j) == (11, 0):
                    dve.wait_ge(gelu_ready, 1)
                    nc.vector.tensor_tensor(tiles(64, 72), tiles(72, 80), tiles(G_RG, G_RG + 8),
                                            ALU.mult).then_inc(rg_y_ready, 1)
                if (n, j) == (11, 7):
                    gate_heads(0)

            link(nc.vector.memset(small[:, 95:96], EPS))
            dve.wait_ge(vectors_landed, 16)
            dve.wait_ge(cond_ready, 1)
            gemm(ab)
            gemm(ab_out)
            drain(ab_out, up0)
            gemm(up0)
            gemm(down0)
            drain(down0, cd)
            gemm(cd)
            gemm(cd_out)
            drain(cd_out, up1)
            gemm(up1)
            gemm(down1)
            drain(down1)
            inverse(final_norm)
            for k in range(KD):
                nc.vector.scalar_tensor_tensor(mixer[:, k], x[:, k], gain[:, final_norm, k:k + 1], inverse_bank[:, 0:T],
                                               ALU.mult, ALU.mult).then_inc(normalised, 1)

        @block.tensor
        def _(pe):
            def sum_mod(group, b, acc=mod_acc):
                pe.wait_ge(mod_folded, group + 1)
                a = accumulator(acc, 0)
                for f in range(4):
                    ins = pe.matmul(b[:, f:f + 1], a[:, f * P:f * P + P], ones[:, 0:1], start=True, stop=True)
                ins.then_inc(mod_reduced, 1)

            def multiply(gm, half, j, k, f):
                operand = hidden if gm in (down0, down1) else acts
                kt, s, b = CHUNK_K * j + k, (j + gm.offset(half)) % RING, bank[4 * half + f]
                wl, wh = low[:, s, k, f * P:f * P + P], high[:, s, k, f * P:f * P + P]
                last = kt == CHUNK_K * gm.n - 1
                if last:
                    pe.matmul(b[:, T:2 * T], wl, operand[:, kt, 0], start=False, stop=False)
                ins = pe.matmul(b[:], wh, operand[:, kt].rearrange("p a t -> p (a t)"),
                                start=(kt == 0), stop=last)
                if not last:
                    ins = pe.matmul(b[:, T:2 * T], wl, operand[:, kt, 0], start=False, stop=False)
                return ins

            def last_chunks(gm, i, half):
                js = (gm.n - 2, gm.n - 1)
                for j in js:
                    pe.wait_ge(*chunk_low(gm, i, half, j))
                for f in range(GROUP):
                    for j in js:
                        for k in range(CHUNK_K):
                            ins = multiply(gm, half, j, k, f)
                        if f == GROUP - 1:
                            ins.then_inc(chunk_used, 1)
                    if f < GROUP - 1:
                        ins.then_inc(tile_multiplied, 1)

            def keep_warm(b, times):
                for _ in range(times):
                    pe.matmul(b[:, 0:T], ident, t("ones"), start=True, stop=True)

            def first_half():
                for q in range(4):
                    for group in (2 * q, 2 * q + 1):
                        wait(pe, mod_ready, group - 1)
                        if group == 7:
                            pe.wait_ge(mod_added, 8 * MOD_CHUNKS - 2)
                            keep_warm(bank[4], 4)
                        sum_mod(group, bank[6 + group % 2], (cross, summed)[group % 2])
                        if group == 7:
                            keep_warm(bank[4], 3)
                    for j in (2 * q, 2 * q + 1):
                        pe.wait_ge(*chunk_low(ab, 0, 0, j))
                        for k in range(CHUNK_K):
                            pe.wait_ge(feed_low, CHUNK_K * j + k + 1)
                            for f in range(GROUP):
                                ins = multiply(ab, 0, j, k, f)
                        ins.then_inc(chunk_used, 1)

            def body(gm, i):
                for half in range(2):
                    groups = gm.groups(i, half)
                    first = isinstance(i, int) and (i, half) == (0, 0)
                    if first and gm is ab:
                        first_half()
                        pe.wait_ge(rms_ready, 1)
                        pe.wait_ge(mod_ready, 8)
                        continue
                    if gm in (ab, cd) and isinstance(i, int):
                        banks_back(gm, 2 * i + half)
                    if first and gm is cd_out:
                        pe.wait_ge(head_done, HEADS_D)
                    if prefilled(gm) and isinstance(i, int) and (i, half) == (0, 1):
                        pe.wait_ge(normed_ready, (norms[gm][0] + 1) * KD)
                    for j in range(gm.n):
                        if is_drained(gm, i, half) and j >= gm.n - 2:
                            if j == gm.n - 2:
                                last_chunks(gm, i, half)
                        else:
                            pe.wait_ge(*chunk_low(gm, i, half, j))
                            if first and gm.fed is None:
                                pe.wait_ge(hidden_low, (0 if gm is down0 else KF) + 2 * j + 2)
                            for k in range(CHUNK_K):
                                if first and gm.fed is not None:
                                    pe.wait_ge(feed_low, KD * gm.fed + CHUNK_K * j + k + 1)
                                for f in range(GROUP):
                                    if j == 0 and k == 0:
                                        wait(pe, tile_out, gm.tiles(i, half) + f - 2 * GROUP + 1)
                                        if f == GROUP - 1:
                                            pe.wait_ge(mod_ready, groups)
                                    ins = multiply(gm, half, j, k, f)
                            ins.then_inc(chunk_used, 1)
                        if gm in (ab, cd) and isinstance(i, int):
                            if j == 3:
                                wait(pe, tile_out, gm.tiles(i, half))
                            mixer_step(gm, 2 * i + half, half, j)
                        r = gm.reduced_after(i, half, j)
                        if r is not None:
                            pe.wait_ge(tile_out, gm.tiles(i, half))
                            sum_mod(groups + r, idle(half, 3))

            def gemm(gm):
                for part in gm.parts():
                    if isinstance(part, int):
                        body(gm, part)
                    else:
                        with pe.Fori(*part) as i:
                            body(gm, i)

            def norm(n):
                pe.wait_ge(tile_out, (ab_out, down0, cd_out, down1)[n - 1].tiles(1, 1))
                keep_warm(bank[1], 3)
                for s in range(2):
                    pe.wait_ge(squares_added, n * (KD - 1))
                    pe.matmul(square_bank[:, s:s + 1], square_acc[:, s * P:s * P + P], mean[:, 0:1],
                              start=True, stop=False)
                    pe.wait_ge(x_squared, 4 + n * KD)
                    ins = pe.matmul(square_bank[:, s:s + 1], square[:, (KD - 1) % 2, s * P:s * P + P],
                                    mean[:, 0:1], start=False, stop=True)
                ins.then_inc(square_sum, 1)
                keep_warm(bank[1], 2)
                pe.wait_ge(diagonal_ready, n)
                for s in range(2):
                    ins = pe.matmul(inverse_bank[:, s * P:s * P + P], ones, diagonal[:, s * P:s * P + P],
                                    start=True, stop=True)
                ins.then_inc(inverse_ready, 1)
                if n != final_norm:
                    keep_warm(bank[1], 4)

            def turn_values(first_tile, b, dst):
                for q in range(4):
                    src = mixer[:, first_tile + 4 * (b % 2) + q, P * (b // 2):P * (b // 2) + P]
                    ins = pe.transpose(dst[:, q * P:q * P + P], src, ident)
                ins.then_inc(v_turned, 1)

            def banks_back(gm, n):
                if gm is ab:
                    if n == 7:
                        pe.wait_ge(v_stored, 4)
                    if 7 <= n <= 10:
                        pe.wait_ge(scores_max, 2 * (n - 6))
                    if 8 <= n <= 11:
                        pe.wait_ge(heads_stored, 2 * (n - 7))
                    return
                for s, count in {2: [(gates_summed, 1)], 3: [(f_rows, 1)], 5: [(rg_sigmoid, 6), (a_stored, 1)],
                                 6: [(rg_sigmoid, 16)], 7: [(p_ready, 2)], 8: [(p_ready, 4)], 9: [(v_stored, 8)],
                                 10: [(head_done, 1)], 11: [(head_done, 3)]}.get(n, ()):
                    pe.wait_ge(s, count)

            def mixer_step(gm, n, half, j):
                if gm is ab:
                    attention_step(n, half, j)
                else:
                    layer1_step(n, half, j)

            def attention_step(n, half, j):
                if n == 6 and j in (3, 5):
                    for q in range(2):
                        b = q if j == 3 else 2 + q
                        if j == 5:
                            pe.wait_ge(v_stored, q + 1)
                        turn_values(V_A, b, idle(half, q))
                if 7 <= n <= 10 and j == 3:
                    for h in (2 * (n - 7), 2 * (n - 7) + 1):
                        pe.wait_ge(probs_ready, h + 1)
                        for q in range(3):
                            ins = pe.transpose(idle(half, h % 2)[:, q * P:q * P + P], probs(h)[:, q * P:q * P + P],
                                               ident)
                        ins.then_inc(probs_turned, 1)
                if 6 <= n <= 9 and j == 3:
                    for h in (2 * (n - 6), 2 * (n - 6) + 1):
                        q, k, s = mixer[:, h], mixer[:, 8 + h], idle(half, 2 + h % 2)
                        pe.matmul(s[:, 0:128], q[:, 0:P], k[:, 0:P], start=True, stop=True)
                        pe.matmul(s[:, 128:384], q[:, P:T], k, start=True, stop=True).then_inc(scores_ready, 1)
                if 7 <= n <= 10 and j == 5:
                    for h in (2 * (n - 7), 2 * (n - 7) + 1):
                        pe.wait_ge(probs_stored, h + 1)
                        pe.wait_ge(v_stored, 4)
                        o = idle(half, h % 2)
                        pe.matmul(o[:, 0:T], v_rows[:, 0, h * P:h * P + P], probs_t(h)[:, 0:256],
                                  start=True, stop=False)
                        pe.matmul(o[:, P:T], v_rows[:, 1, h * P:h * P + P], probs_t(h)[:, 256:384],
                                  start=False, stop=True).then_inc(heads_out, 1)
                if 6 <= n <= 9 and j == 6:
                    pe.wait_ge(scores_max, 2 * (n - 6) + 2)

            def rg_gate_products(gs, half):
                for g, b in gs:
                    pe.wait_ge(rg_conv_ready, g + 1)
                    for n in range(2):
                        ins = pe.matmul(idle(half, b)[:, n * T:n * T + T], rg_blocks[:, n, g], mixer[:, 64 + g],
                                        start=True, stop=True)
                    ins.then_inc(rg_products, 1)

            def head_products(h):
                w, c0 = weighted(h), head_bank(h, 0)
                pe.matmul(c0[:, 0:T], ones, w[:, 0:256], start=True, stop=False)
                pe.matmul(c0[:, P:T], ones, w[:, 256:384], start=False, stop=True)
                pe.matmul(c0[:, T:2 * T], select[0:4, h], row(3), start=True, stop=True)
                for e in range(TILES_D):
                    c = (2 * h + e) * P
                    o = head_bank(h, 1)[:, e * T:e * T + T]
                    pe.matmul(o, v_rows[:, 0, c:c + P], w[:, 0:256], start=True, stop=False)
                    ins = pe.matmul(o[:, P:T], v_rows[:, 1, c:c + P], w[:, 256:384], start=False, stop=True)
                ins.then_inc(num_ready, 1)

            def layer1_step(n, half, j):
                if (n, j) == (1, 3):
                    pe.wait_ge(gates_split, 1)
                    for k in range(KD):
                        ins = pe.matmul(idle(half, 0)[0:16], gates_w[:, k].rearrange("p a n -> p (a n)"),
                                        acts[:, k].rearrange("p a t -> p (a t)"), start=(k == 0),
                                        stop=(k == KD - 1))
                    ins.then_inc(gates_done, 1)
                if (n, j) == (2, 3):
                    pe.wait_ge(gates_summed, 1)
                    pe.wait_ge(futures_landed, 16)
                    for q in range(2):
                        ins = pe.matmul(idle(half, 0)[0:4, q * T:q * T + T], pick[:, 4 * q:4 * q + 4], gate_sums,
                                        start=True, stop=True)
                    ins.then_inc(gates_rows, 1)
                if (n, j) == (4, 3):
                    pe.wait_ge(rg_landed, 16)
                    rg_gate_products(((0, 0), (1, 1), (2, 2)), half)
                if (n, j) == (4, 5):
                    pe.wait_ge(m_rows, 1)
                    for s in range(2):
                        ins = pe.matmul(idle(half, 3)[:, 4 * s:4 * s + 4], row(0)[:, s * P:s * P + P],
                                        ident[0:4, 0:4], start=True, stop=True)
                    ins.then_inc(a_turned, 1)
                if (n, j) == (5, 3):
                    rg_gate_products(((3, 0), (4, 1), (5, 2)), half)
                if (n, j) == (5, 6):
                    pe.wait_ge(rg_sigmoid, 10)
                    rg_gate_products(((6, 0), (7, 1)), half)
                if n in (6, 7) and j == 3:
                    pair = (2 * (n - 6), 2 * (n - 6) + 1)
                    pe.wait_ge(futures_landed, 16)
                    for q, h in enumerate(pair):
                        ins = pe.matmul(idle(half, 0)[:, q * T:q * T + T], select[0:4, h], row(1),
                                        start=True, stop=True)
                    ins.then_inc(m_spread, 1)
                    for q, h in enumerate(pair):
                        for a, b, s in ((0, 256, 0), (256, 384, P)):
                            for d in range(TILES_D):
                                qt, kt = mixer[:, Q_D + 2 * h + d], mixer[:, K_D + 2 * h + d]
                                ins = pe.matmul(idle(half, 1 + q)[:, a:b], kt[:, s:s + P], qt[:, s:T],
                                                start=(d == 0), stop=(d == 1))
                        ins.then_inc(qk_ready, 1)
                if n == 8 and j in (3, 5):
                    for b in ((0, 1) if j == 3 else (2, 3)):
                        turn_values(V_D, b, idle(half, b))
                if (n, j) == (9, 3):
                    pe.wait_ge(m_exp, 1)
                    pe.wait_ge(p_ready, HEADS_D)
                    head_products(0)
                if (n, j) == (10, 3):
                    head_products(1)
                if (n, j) == (10, 4):
                    head_products(2)
                if (n, j) == (11, 3):
                    head_products(3)

            pe.wait_ge(tables_landed, 48)
            for j in range(4):
                pe.wait_ge(x_squared, j + 1)
                for q in range(4):
                    k = 4 * j + q
                    ins = pe.matmul(square_bank[:, 0:T], mean, mixer[:, 16 + k], start=(k == 0), stop=(k == KD - 1))
            ins.then_inc(square_sum, 1)
            gemm(ab)
            gemm(ab_out)
            norm(1)
            gemm(up0)
            gemm(down0)
            norm(2)
            gemm(cd)
            gemm(cd_out)
            norm(3)
            gemm(up1)
            gemm(down1)
            norm(final_norm)


def _chunks(w):
    k, n = w.shape
    return w.reshape(k // 256, 2, 128, n // 512, 512).transpose(3, 0, 2, 1, 4).reshape(n // 512, k // 256, 128, 1024)


AB_ORDER = [0, 1, 2, 3, 4, 5, 8, 10, 6, 9, 11, 7]
CD_ORDER = [0, 1, 4, 5, 6, 7, 8, 9, 2, 3, 10, 11]

FIRST_MODS = [4, 0, 5, 1, 6, 2, 7, 3]


def kernel(**inputs):
    import numpy as np
    import concourse.bacc as bacc
    from concourse.bass_utils import run_bass_kernel_spmd

    a = {k: np.asarray(w) for k, w in inputs.items()}

    def columns(vector):
        return vector.reshape(-1, 128).T

    def flat_chunks(w):
        return _chunks(w).reshape(-1, 128, 1024)

    def pairs(w1, w3):
        return np.stack([_chunks(w1), _chunks(w3)], axis=1).reshape(-1, 128, 1024)

    cd_w = a["cd_w_in"][0]
    gates_at = cd_w.shape[1] - 8
    weights = np.concatenate([
        _chunks(a["ab_w_in"][0])[AB_ORDER].reshape(-1, 128, 1024), flat_chunks(a["ab_w_out"][0]),
        pairs(a["ffn_w1"][0], a["ffn_w3"][0]), flat_chunks(a["ffn_w2"][0]),
        _chunks(cd_w[:, :gates_at])[CD_ORDER].reshape(-1, 128, 1024), flat_chunks(a["cd_w_out"][0]),
        pairs(a["ffn_w1"][1], a["ffn_w3"][1]), flat_chunks(a["ffn_w2"][1]),
    ])
    mod_0 = _chunks(a["mod_w"][0])
    mod_weights = np.concatenate([mod_0[FIRST_MODS].reshape(-1, 128, 1024), mod_0[8:].reshape(-1, 128, 1024),
                                  flat_chunks(a["mod_w"][1])])
    mod_b = a["mod_b"].reshape(-1, 512)
    mod_b = np.concatenate([mod_b[FIRST_MODS], mod_b[8:]])
    vectors = np.concatenate([
        columns(a["c"][0]), columns(mod_b.reshape(-1)),
        columns(np.concatenate([a["norm_mix_g"][0], a["norm_ffn_g"][0], a["norm_mix_g"][1],
                                a["norm_ffn_g"][1], a["final_norm_g"]])),
        a["ab_conv_w"][0].reshape(3, 8, 128).transpose(2, 1, 0).reshape(128, 24),
        a["rg_conv_w"][0].reshape(4, 8, 128).transpose(2, 1, 0).reshape(128, 32),
        columns(a["rg_conv_b"][0]), columns(a["rg_ba"][0]), columns(a["rg_bx"][0]), columns(a["rg_lambda"][0]),
        cd_w[:, gates_at:].reshape(16, 128, 8).transpose(1, 0, 2).reshape(128, 128),
    ], axis=1)
    gate_b = np.ascontiguousarray(a["cd_gate_b"].reshape(2, 4).T)
    rg_w = np.stack([a["rg_wa"][0], a["rg_wx"][0]]).transpose(2, 0, 1, 3).reshape(128, 2048)

    n = np.arange(128)
    back = n[:, None] - n[None, :]
    causal = np.where(back >= 0, -back, -1e34).astype(np.float32)
    distance = np.concatenate([causal, -(back + 128).astype(np.float32), causal], axis=1)
    later = np.where(n[:, None] > n[None, :], 1e30, 0.0).astype(np.float32)
    future = np.concatenate([later, np.zeros((128, 128), np.float32), later], axis=1)
    select = np.zeros((128, 4, 128), np.float32)
    for h in range(4):
        select[h, h] = 1.0
    tables = np.concatenate([np.eye(128, dtype=np.float32), np.ones((128, 256), np.float32),
                             np.full((128, 128), 1 / D, np.float32)], axis=1)
    pick = np.zeros((128, 8), np.float32)
    pick[n[:16], n[:16] % 8] = 1.0
    futures = np.concatenate([future, select.reshape(128, 512), pick], axis=1)

    arrays = {"x_t": a["x"][0].T, "weights": weights, "mod_weights": mod_weights, "vectors": vectors,
              "tables": tables, "distances": distance, "futures": futures, "gate_b": gate_b, "rg_w": rg_w}
    arrays = {k: np.ascontiguousarray(w) for k, w in arrays.items()}
    nc = bacc.Bacc("TRN2", target_bir_lowering=False, num_devices=1, dynamic_dma_scratch_size=1024)
    args = [nc.dram_tensor(k, w.shape, F32, kind="ExternalInput").ap() for k, w in arrays.items()]
    out = nc.dram_tensor("out_t", (D, T), F32, kind="ExternalOutput").ap()
    trunk(nc, *args, out)
    r = run_bass_kernel_spmd(nc, [arrays], core_ids=[0])
    return np.ascontiguousarray(r.results[0]["out_t"].T)[None]
```
